# Optimizing a Trainium2 kernel written in Bass

```python
import jax
import jax.numpy as jnp
from jax import lax
import numpy as np

D_MODEL = 1024
BATCH = 1
SEQ = 1024
DEPTH = 1
DEC_BATCH = 8
DEC_SEQ = 8
PAST_LEN = 2048
PAGE_SIZE = 128

HEAD_DIM = 64
DSW_GROUPS = ((128, 1), (512, 4), (2048, 16))
DSW_HPG = 4
DSW_HEADS = DSW_HPG * len(DSW_GROUPS)
DSW_WIDTH = DSW_HEADS * HEAD_DIM
DSW_OUT = DSW_HPG * HEAD_DIM
SB_HEADS = 8
SB_WIDTH = SB_HEADS * HEAD_DIM
SB_BIAS_INIT = -6.0
MEM_LEN = 256
MEM_HEADS = 4
MEM_WIDTH = MEM_HEADS * HEAD_DIM
D_FF = 4 * D_MODEL
IN_WIDTH = 3 * DSW_WIDTH + 3 * SB_WIDTH + 2 * D_MODEL
REL_BUCKETS = 32
REL_MAX_DIST = 2048
Q_BLOCK = 128
EPS = 1e-6
NEG_INF = -1e30
POOL_NUM, POOL_DEN = 5, 4

kernel_name = 'hybrid_dilated_stickbreaking_decoder_step'

def rms_norm(x, gain):
    xf = x.astype(jnp.float32)
    y = xf * lax.rsqrt(jnp.mean(xf * xf, axis=-1, keepdims=True) + EPS)
    return (y * gain.astype(jnp.float32)).astype(x.dtype)

def t5_causal_bucket(dist):
    dist = np.asarray(dist, np.int64)
    max_exact = REL_BUCKETS // 2
    safe = np.maximum(dist, max_exact).astype(np.float32)
    large = max_exact + (np.log(safe / max_exact) / np.log(REL_MAX_DIST / max_exact)
                         * (REL_BUCKETS - max_exact)).astype(np.int64)
    large = np.minimum(large, REL_BUCKETS - 1)
    return np.where(dist < max_exact, dist, large).astype(np.int32)

def dsw_group_biases(rel_bias):
    biases = []
    for g, (window, dil) in enumerate(DSW_GROUPS):
        buckets = t5_causal_bucket(np.arange(window // dil + 1) * dil)
        biases.append(rel_bias[buckets][:, g * DSW_HPG:(g + 1) * DSW_HPG].T.astype(jnp.float32))
    return biases

def group_slice(g):
    return slice(g * DSW_HPG, (g + 1) * DSW_HPG)

def split_in(h, w_in):
    b, t, _ = h.shape
    sizes = [DSW_WIDTH] * 3 + [SB_WIDTH] * 3 + [D_MODEL] * 2
    offs = [int(o) for o in np.cumsum(sizes)[:-1]]
    qa, ka, va, qb, kb, vb, ga, gb = jnp.split(h @ w_in, offs, axis=-1)
    heads = lambda z, n: z.reshape(b, t, n, HEAD_DIM)
    return (heads(qa, DSW_HEADS), heads(ka, DSW_HEADS), heads(va, DSW_HEADS),
            heads(qb, SB_HEADS), heads(kb, SB_HEADS), heads(vb, SB_HEADS), ga, gb)

def sweep_query_blocks(fn, q, qpos):
    batch, tq = q.shape[:2]
    if tq <= Q_BLOCK or tq % Q_BLOCK:
        return fn(q, qpos)
    nb = tq // Q_BLOCK
    q_blocks = jnp.swapaxes(q.reshape(batch, nb, Q_BLOCK, *q.shape[2:]), 0, 1)
    out = lax.map(lambda a: fn(a[0], a[1]), (q_blocks, qpos.reshape(nb, Q_BLOCK)))
    return jnp.swapaxes(out, 0, 1).reshape(batch, tq, *out.shape[3:])

def dsw_block(q, qrow, groups, biases):
    scale = HEAD_DIM ** -0.5
    outs, lses = [], []
    for g, ((window, dil), (k_ext, v_ext, off), bias) in enumerate(zip(DSW_GROUPS, groups, biases)):
        dist = jnp.arange(window // dil + 1, dtype=jnp.int32) * dil
        idx = off + qrow[:, None] - dist[None, :]
        valid = idx >= 0
        idx = jnp.maximum(idx, 0)
        kg = jnp.take(k_ext, idx, axis=1)
        vg = jnp.take(v_ext, idx, axis=1)
        qg = q[:, :, group_slice(g)]
        s = jnp.einsum('bqhd,bqmhd->bhqm', qg, kg).astype(jnp.float32) * scale + bias[None, :, None, :]
        s = jnp.where(valid[None, None], s, NEG_INF)
        lse = jax.nn.logsumexp(s, axis=-1)
        p = jnp.exp(s - lse[..., None]).astype(vg.dtype)
        outs.append(jnp.einsum('bhqm,bqmhd->bqhd', p, vg).astype(jnp.float32))
        lses.append(jnp.swapaxes(lse, 1, 2))
    w = jax.nn.softmax(jnp.stack(lses), axis=0)
    o = jnp.sum(w[..., None] * jnp.stack(outs), axis=0)
    return o.astype(q.dtype)

def sb_block(q, qpos, k, v, kpos, sb_bias):
    z = (jnp.einsum('bqhd,bkhd->bhqk', q, k).astype(jnp.float32) * HEAD_DIM ** -0.5
         + sb_bias.astype(jnp.float32)[None, :, None, None])
    causal = (kpos[None, :] < qpos[:, None])[None, None]
    log_1mb = jnp.where(causal, jax.nn.log_sigmoid(-z), 0.0)
    suffix = lax.cumsum(log_1mb, axis=3, reverse=True) - log_1mb
    a = jnp.where(causal, jnp.exp(jax.nn.log_sigmoid(z) + suffix), 0.0)
    return jnp.einsum('bhqk,bkhd->bqhd', a.astype(v.dtype), v)

def memory_kv(mem, norm_mem, w_ck, w_cv):
    b, m, _ = mem.shape
    hm = rms_norm(mem, norm_mem)
    k = (hm @ w_ck).reshape(b, m, MEM_HEADS, HEAD_DIM)
    v = (hm @ w_cv).reshape(b, m, MEM_HEADS, HEAD_DIM)
    return k, v

def cross_attend(h, mem_k, mem_v, w_cq, w_co):
    b, t, _ = h.shape
    q = (h @ w_cq).reshape(b, t, MEM_HEADS, HEAD_DIM)
    s = jnp.einsum('bthd,bmhd->bhtm', q, mem_k).astype(jnp.float32) * HEAD_DIM ** -0.5
    p = jax.nn.softmax(s, axis=-1).astype(mem_v.dtype)
    o = jnp.einsum('bhtm,bmhd->bthd', p, mem_v)
    return o.reshape(b, t, MEM_WIDTH) @ w_co

def layer_tail(x, o_a, o_b, g_a, g_b, mem_k, mem_v, w_branch_a, w_branch_b, w_out,
               norm_cross, w_cq, w_co, norm_mlp, w_up, w_down):
    b, t, _ = x.shape
    branch_a = o_a.reshape(b, t, DSW_OUT) @ w_branch_a
    branch_b = o_b.reshape(b, t, SB_WIDTH) @ w_branch_b
    merged = jax.nn.sigmoid(g_a) * branch_a + jax.nn.sigmoid(g_b) * branch_b
    x = x + merged @ w_out
    x = x + cross_attend(rms_norm(x, norm_cross), mem_k, mem_v, w_cq, w_co)
    hid = jax.nn.relu(rms_norm(x, norm_mlp) @ w_up)
    return x + (hid * hid) @ w_down

def setup_inputs(seed: int = 0) -> dict:
    key = jax.random.key(seed)
    keys = iter(jax.random.split(key, 40))

    def normal(shape, scale=1.0):
        return jax.random.normal(next(keys), shape, jnp.float32) * scale

    def gain(shape):
        return 1.0 + normal(shape, 0.05)

    n_pages = PAST_LEN // PAGE_SIZE
    n_pool = (DEC_BATCH * n_pages * POOL_NUM) // POOL_DEN
    inputs = {}
    inputs['x_prompt'] = normal((BATCH, SEQ, D_MODEL))
    inputs['x_sample'] = normal((DEC_BATCH, DEC_SEQ, D_MODEL))
    inputs['mem_prompt'] = normal((BATCH, MEM_LEN, D_MODEL))
    for g, (window, _) in enumerate(DSW_GROUPS):
        keep = min(window, PAST_LEN)
        for kv in ('k', 'v'):
            inputs[f'cache_win{g + 1}_{kv}'] = normal((DEPTH, DEC_BATCH, keep, DSW_HPG, HEAD_DIM))
    inputs['cache_sb_k'] = normal((DEPTH, n_pool, PAGE_SIZE, SB_HEADS, HEAD_DIM))
    inputs['cache_sb_v'] = normal((DEPTH, n_pool, PAGE_SIZE, SB_HEADS, HEAD_DIM))
    inputs['cache_mem_k'] = normal((DEPTH, DEC_BATCH, MEM_LEN, MEM_HEADS, HEAD_DIM))
    inputs['cache_mem_v'] = normal((DEPTH, DEC_BATCH, MEM_LEN, MEM_HEADS, HEAD_DIM))
    perm = jax.random.permutation(next(keys), n_pool)[:DEC_BATCH * n_pages]
    inputs['page_table'] = perm.reshape(DEC_BATCH, n_pages).astype(jnp.int32)
    inputs['norm_mix'] = gain((DEPTH, D_MODEL))
    inputs['w_in'] = normal((DEPTH, D_MODEL, IN_WIDTH), D_MODEL ** -0.5)
    inputs['w_branch_a'] = normal((DEPTH, DSW_OUT, D_MODEL), DSW_OUT ** -0.5)
    inputs['w_branch_b'] = normal((DEPTH, SB_WIDTH, D_MODEL), SB_WIDTH ** -0.5)
    inputs['w_out'] = normal((DEPTH, D_MODEL, D_MODEL), D_MODEL ** -0.5)
    inputs['rel_bias'] = normal((REL_BUCKETS, DSW_HEADS), 0.2)
    inputs['sb_bias'] = SB_BIAS_INIT + normal((DEPTH, SB_HEADS), 0.1)
    inputs['norm_cross'] = gain((DEPTH, D_MODEL))
    inputs['norm_mem'] = gain((DEPTH, D_MODEL))
    inputs['w_cq'] = normal((DEPTH, D_MODEL, MEM_WIDTH), D_MODEL ** -0.5)
    inputs['w_ck'] = normal((DEPTH, D_MODEL, MEM_WIDTH), D_MODEL ** -0.5)
    inputs['w_cv'] = normal((DEPTH, D_MODEL, MEM_WIDTH), D_MODEL ** -0.5)
    inputs['w_co'] = normal((DEPTH, MEM_WIDTH, D_MODEL), MEM_WIDTH ** -0.5)
    inputs['norm_mlp'] = gain((DEPTH, D_MODEL))
    inputs['w_up'] = normal((DEPTH, D_MODEL, D_FF), D_MODEL ** -0.5)
    inputs['w_down'] = normal((DEPTH, D_FF, D_MODEL), D_FF ** -0.5)
    inputs['norm_final'] = gain((D_MODEL,))
    return inputs

def reference(x_prompt, x_sample, mem_prompt,
              cache_win1_k, cache_win1_v, cache_win2_k, cache_win2_v, cache_win3_k, cache_win3_v,
              cache_sb_k, cache_sb_v, cache_mem_k, cache_mem_v, page_table,
              norm_mix, w_in, w_branch_a, w_branch_b, w_out, rel_bias, sb_bias,
              norm_cross, norm_mem, w_cq, w_ck, w_cv, w_co,
              norm_mlp, w_up, w_down, norm_final):
    biases = dsw_group_biases(rel_bias)
    win_caches = ((cache_win1_k, cache_win1_v), (cache_win2_k, cache_win2_v), (cache_win3_k, cache_win3_v))
    t_prompt = x_prompt.shape[1]
    n_dec, t_new = x_sample.shape[:2]
    past = page_table.shape[1] * cache_sb_k.shape[2]
    prompt_rows = jnp.arange(t_prompt, dtype=jnp.int32)
    new_rows = jnp.arange(t_new, dtype=jnp.int32)
    all_pos = jnp.arange(past + t_new, dtype=jnp.int32)

    prompt_lists = [[] for _ in range(10)]
    sample_lists = [[] for _ in range(8)]
    xp, xs = x_prompt, x_sample
    for layer in range(DEPTH):
        tail_w = (w_branch_a[layer], w_branch_b[layer], w_out[layer], norm_cross[layer],
                  w_cq[layer], w_co[layer], norm_mlp[layer], w_up[layer], w_down[layer])
        sbb = sb_bias[layer]

        qa, ka, va, qb, kb, vb, ga, gb = split_in(rms_norm(xp, norm_mix[layer]), w_in[layer])
        p_groups = tuple((ka[:, :, group_slice(g)], va[:, :, group_slice(g)], 0) for g in range(len(DSW_GROUPS)))
        o_a = sweep_query_blocks(lambda q, r: dsw_block(q, r, p_groups, biases), qa, prompt_rows)
        o_b = sweep_query_blocks(lambda q, p: sb_block(q, p, kb, vb, prompt_rows, sbb), qb, prompt_rows)
        mk, mv = memory_kv(mem_prompt, norm_mem[layer], w_ck[layer], w_cv[layer])
        xp = layer_tail(xp, o_a, o_b, ga, gb, mk, mv, *tail_w)
        for g, (window, _) in enumerate(DSW_GROUPS):
            keep = min(window, t_prompt)
            prompt_lists[2 * g].append(p_groups[g][0][:, t_prompt - keep:])
            prompt_lists[2 * g + 1].append(p_groups[g][1][:, t_prompt - keep:])
        prompt_lists[6].append(kb)
        prompt_lists[7].append(vb)
        prompt_lists[8].append(mk)
        prompt_lists[9].append(mv)

        qa, ka, va, qb, kb, vb, ga, gb = split_in(rms_norm(xs, norm_mix[layer]), w_in[layer])
        s_groups = []
        for g, (ck, cv) in enumerate(win_caches):
            keep = ck.shape[2]
            k_ext = jnp.concatenate([ck[layer], ka[:, :, group_slice(g)]], axis=1)
            v_ext = jnp.concatenate([cv[layer], va[:, :, group_slice(g)]], axis=1)
            s_groups.append((k_ext, v_ext, keep))
            sample_lists[2 * g].append(k_ext[:, k_ext.shape[1] - keep:])
            sample_lists[2 * g + 1].append(v_ext[:, v_ext.shape[1] - keep:])
        s_groups = tuple(s_groups)
        o_a = sweep_query_blocks(lambda q, r: dsw_block(q, r, s_groups, biases), qa, new_rows)
        k_past = cache_sb_k[layer][page_table].reshape(n_dec, past, SB_HEADS, HEAD_DIM)
        v_past = cache_sb_v[layer][page_table].reshape(n_dec, past, SB_HEADS, HEAD_DIM)
        k_all = jnp.concatenate([k_past, kb], axis=1)
        v_all = jnp.concatenate([v_past, vb], axis=1)
        o_b = sweep_query_blocks(lambda q, p: sb_block(q, p, k_all, v_all, all_pos, sbb), qb, past + new_rows)
        xs = layer_tail(xs, o_a, o_b, ga, gb, cache_mem_k[layer], cache_mem_v[layer], *tail_w)
        sample_lists[6].append(kb)
        sample_lists[7].append(vb)

    y_prompt = rms_norm(xp, norm_final)
    y_sample = rms_norm(xs, norm_final)
    prompt_state = [jnp.stack(s) for s in prompt_lists]
    sample_state = [jnp.stack(s) for s in sample_lists]
    return (y_prompt, y_sample, *prompt_state, *sample_state)


_drawn_inputs = setup_inputs


def setup_inputs(seed=0):
    import zlib

    import numpy as np

    out = dict(_drawn_inputs(seed))
    spreads = {}
    factors = {'rel_bias': 4.442, 'sb_bias': 8.0, 'norm_cross': 8.0}
    for name, (base, spread) in spreads.items():
        noise = np.random.default_rng([zlib.crc32(name.encode()), seed]).standard_normal(out[name].shape)
        drawn = base * np.exp(spread * noise) if base else spread * noise
        out[name] = jnp.asarray(drawn.astype(out[name].dtype))
    for name, factor in factors.items():
        out[name] = (out[name] * factor).astype(out[name].dtype)
    return out
```

```python
from contextlib import ExitStack

import numpy as np

import concourse.bass as bass
from concourse import mybir

F32 = mybir.dt.float32
I32 = mybir.dt.int32
ALU = mybir.AluOpType
ACT = mybir.ActivationFunctionType
AX = mybir.AxisListType

P = 128
D = 1024
KT = D // P
SEQ = 1024
NB = 8
NQ = 8
TOK = SEQ + NB * NQ
TT = SEQ // P + 1
HD = 64
GROUPS = ((128, 1), (512, 4), (2048, 16))
HPG = 4
GW = HPG * HD
SBH = 8
SBW = SBH * HD
MEM = 256
PAGES = 16
F = 4096
EPS = 1e-6
NEG = -1e30
BIG = 30.0
LOW = -3.0e38
BUCKETS = 32
MAX_DIST = 2048
NTAPS = 129


def bucket_runs(dil):
    dist = np.arange(NTAPS, dtype=np.int64) * dil
    exact = BUCKETS // 2
    safe = np.maximum(dist, exact).astype(np.float32)
    large = exact + (np.log(safe / exact) / np.log(MAX_DIST / exact) * (BUCKETS - exact)).astype(np.int64)
    b = np.where(dist < exact, dist, np.minimum(large, BUCKETS - 1))
    runs, start = [], 0
    for m in range(1, NTAPS + 1):
        if m == NTAPS or b[m] != b[start]:
            runs.append((start, m, int(b[start])))
            start = m
    return runs


def hybrid_decoder_kernel(nc, ins, outs, scratch):
    (x_prompt, x_sample, mem_prompt, w1k, w1v, w2k, w2v, w3k, w3v, sbk, sbv, memk, memv, page_table,
     norm_mix, w_in, w_ba, w_bb, w_out, rel_bias, sb_bias, norm_cross, norm_mem, w_cq, w_ck, w_cv, w_co,
     norm_mlp, w_up, w_down, norm_final) = ins
    y_p, y_s = outs[0:2]
    p_win = outs[2:8]
    p_sbk, p_sbv, p_memk, p_memv = outs[8:12]
    s_win = outs[12:18]
    s_sbk, s_sbv = outs[18:20]
    win_cache = (w1k, w1v, w2k, w2v, w3k, w3v)
    bias_lines, tap_rows, line_copies = scratch

    REACH = [min(w // P + 1, SEQ // P) for w, _ in GROUPS]
    SEG = [0, REACH[0] * P, (REACH[0] + REACH[1]) * P, sum(REACH) * P]
    LINE = [(n + 1) * P for n in REACH]

    def cols(w, c0, n, k=KT, k0=0):
        return w[0].rearrange("(k p) n -> p k n", p=P)[:, k0:k0 + k, c0:c0 + n]

    slots, slot_of = [], {}

    def slot(key, parts):
        slot_of[key] = len(slots)
        slots.append(parts)

    SLOTW = 2 * P
    offs = {}
    at = 0
    for name, width in (("qa", 768), ("ka", 768), ("va", 768), ("qb", 512), ("kb", 512), ("vb", 512),
                        ("ga", D), ("gb", D)):
        offs[name] = at
        at += width
    for name, n in (("qa", 3), ("ka", 3), ("va", 3), ("qb", 2), ("kb", 2), ("vb", 2)):
        for s in range(n):
            slot((name, s), [(cols(w_in, offs[name] + s * SLOTW, SLOTW), KT, SLOTW)])
    for s in range(4):
        slot(("ga", s), [(cols(w_in, offs["ga"] + s * SLOTW, SLOTW), KT, SLOTW)])
        slot(("gb", s), [(cols(w_in, offs["gb"] + s * SLOTW, SLOTW), KT, SLOTW)])
        slot(("br", s), [(cols(w_ba, s * SLOTW, SLOTW, 2), 2, SLOTW), (cols(w_bb, s * SLOTW, SLOTW, 4), 4, SLOTW)])
    for s in range(4):
        slot(("wo", s), [(cols(w_out, s * SLOTW, SLOTW), KT, SLOTW)])
    slot(("ck", 0), [(cols(w_ck, 0, SLOTW), KT, SLOTW)])
    slot(("cv", 0), [(cols(w_cv, 0, SLOTW), KT, SLOTW)])
    slot(("cq", 0), [(cols(w_cq, 0, SLOTW), KT, SLOTW)])
    slot(("co", 0), [(cols(w_co, 0, D, 2), 2, D)])
    NC = F // 512
    for c in range(NC + 1):
        for s in range(2):
            if c < NC:
                slot(("up", c, s), [(cols(w_up, c * 512 + s * SLOTW, SLOTW), KT, SLOTW)])
        for s in range(2):
            if c >= 1:
                slot(("dn", c - 1, s), [(cols(w_down, s * 512, 512, 4, 4 * (c - 1)), 4, 512)])
    RING = 3

    units = [(("nm", 0), "v")]
    for name, n, e in (("qa", 6, "a"), ("ka", 6, "a"), ("va", 6, "a"), ("qb", 4, "a"), ("kb", 4, "a"), ("vb", 4, "a")):
        units += [((name, i), e) for i in range(n)]
    for i in range(KT):
        units += [(("ga", i), "a"), (("ba", i), "v"), (("gb", i), "a"), (("bb", i), "v")]
    units += [(("wo", i), "v") for i in range(KT)]
    units += [(("nm", 3), "v")] + [(("ck", i), "a") for i in range(2)] + [(("cv", i), "a") for i in range(2)]
    units += [(("nm", 1), "v")] + [(("cq", i), "a") for i in range(2)]
    units += [(("co", i), "v") for i in range(KT)]
    units += [(("nm", 2), "v")]
    for c in range(NC):
        units += [(("up", c, i), "a") for i in range(4)]
        if c >= 1:
            units += [(("dn", c - 1, i), "v") for i in range(KT)]
    units += [(("dn", NC - 1, i), "v") for i in range(KT)]
    units += [(("nm", 4), "v")]
    unit_no = {k: i for i, (k, _) in enumerate(units)}
    count = {"a": 0, "v": 0}
    emptied = []
    for _, e in units:
        count[e] += 1
        emptied.append((e, count[e]))

    NEWK = NB * NQ
    SAMPLE_KEYS = [P, 512, 1024]
    WINW = sum(SAMPLE_KEYS) + 3 * NEWK
    sm = [("sw", h) for h in range(2)]
    sm += [("pw", h, t) for h in range(HPG) for t in range(SEQ // P)]
    sm += [("sx", h) for h in range(2)]
    sm += [("px", h, t) for h in range(HPG) for t in range(SEQ // P)]
    sm_no = {k: i for i, k in enumerate(sm)}

    def blocks(u):
        k = sm[u]
        if k[0] == "pw":
            return [(g, b, P) for g in range(3) for b in range(max(0, k[2] + 1 - REACH[g]), k[2] + 1)]
        if k[0] == "sw":
            return ([(0, 0, P)] + [(1, r, P) for r in range(4)] + [(2, r, P) for r in range(8)]
                    + [(g, -1, NEWK) for g in range(3)])
        return [(0, 0, P), (0, 1, P)]

    def width(u):
        return sum(w for _, _, w in blocks(u))

    def quads(u):
        b = blocks(u)
        return [b[i:i + 4] for i in range(0, len(b), 4)]

    quad_base = [0]
    for u in range(len(sm)):
        quad_base.append(quad_base[-1] + len(quads(u)))

    psteps = [("p", h, c, b) for h in range(SBH) for c in range(2) for b in range(4 * c + 3, -1, -1)]
    ssteps = [("s", b, g) for b in range(NB) for g in range(-1, 4)]
    steps = []
    j = 0
    for i, s in enumerate(psteps):
        steps.append(s)
        while j < len(ssteps) and (j + 1) * len(psteps) <= (i + 1) * len(ssteps):
            steps.append(ssteps[j])
            j += 1
    NS = len(steps)
    last_of = {}
    for i, s in enumerate(steps):
        last_of[("p", s[1], s[2]) if s[0] == "p" else ("s", s[1])] = i

    def lo_of(s):
        return max(0, s[3] * P - s[2] * 512)

    def span(s):
        return 512 - lo_of(s) if s[0] == "p" else 256 if s[2] >= 0 else NEWK

    def rows(s):
        return NEWK if s[0] == "s" and s[2] < 0 else P

    def diagonal(s):
        return s[0] == "p" and s[3] >= 4 * s[2]

    with ExitStack() as ctx:
        def sb(name, shape, dt=F32):
            return ctx.enter_context(nc.sbuf_tensor(name, shape, dt))

        def sem(name):
            return ctx.enter_context(nc.semaphore(name))

        psum = ctx.enter_context(nc.psum_tensor("psum", [P, 8 * 512], F32))

        def bank(i, n=1):
            return psum[:, i * 512:(i + n) * 512]

        RX = sb("RX", [P, KT * TOK])
        RH = sb("RH", [P, KT * TOK])
        RR = sb("RR", [P, RING * 2048])
        RQ = sb("RQ", [P, 19968])
        RO = sb("RO", [P, 6 * TOK])

        def cut(region, at, *dims):
            n = int(np.prod(dims))
            v = region[:, at:at + n]
            if len(dims) == 2:
                return v.rearrange("p (a b) -> p a b", a=dims[0])
            if len(dims) == 3:
                return v.rearrange("p (a b c) -> p a b c", a=dims[0], b=dims[1])
            if len(dims) == 4:
                return v.rearrange("p (a b c d) -> p a b c d", a=dims[0], b=dims[1], c=dims[2])
            return v

        xT = cut(RX, 0, KT, TOK)
        hT = cut(RH, 0, KT, TOK)
        ring = cut(RR, 0, RING, 2048)
        oaT = cut(RO, 0, 2, TOK)
        obT = cut(RO, 2 * TOK, 4, TOK)
        qaT = cut(RQ, 0, 6, TOK)
        kaT = cut(RQ, 6 * TOK, 6, TOK)
        va = cut(RQ, 12 * TOK, TT, 768)
        vt = cut(RX, 0, 2, TOK)
        kn = cut(RX, 2 * TOK, 2, TT, GW)
        PTs = cut(RO, 2 * TOK, 4, 512)
        onat = cut(RO, 2 * TOK + 2048, 8, GW)
        qblk = cut(RO, 2 * TOK + 2048, 6, NB, 32)
        KVC = 1280
        OLDK = sum(SAMPLE_KEYS)
        kvw = cut(RX, 0, 3, KVC)
        ktw = cut(RX, 3 * KVC, 2, 512)
        pS = cut(RX, 3 * KVC + 1024, WINW)
        Ts = cut(RX, 6784, OLDK)
        TsN = cut(RO, 2 * TOK + 2048 + 6 * NB * 32, 2, 3, NEWK)
        Th = cut(RX, 0, 2, 1920)
        pP = cut(RX, 3840, 2, 1920)
        AT = KT * TOK + 2 * D
        taps = RQ[0:12, AT:AT + 3 * NTAPS].rearrange("p (g m) -> p g m", g=3)
        relT = RQ[0:12, AT + 387:AT + 387 + BUCKETS]
        LN = AT + 420
        lines = RQ[0:12, LN:LN + sum(LINE)]
        rowt = cut(RQ, LN + 2304, 3, NTAPS)
        RP1 = cut(RQ, LN + 2692, 144)
        RP2 = cut(RQ, LN + 2836, 528)
        ohw = cut(RQ, LN + 3364, 16, 8)
        oh = cut(RQ, LN + 3492, 8)
        selr = cut(RQ, LN + 3500, 8)
        T2 = cut(RQ, LN + 3508, 520)
        T1 = cut(RQ, LN + 4028, 136)
        bsel = cut(RQ, LN + 4164, 2, NB)
        nw3 = cut(RQ, LN + 4180, 8)
        qbT = cut(RQ, 0, 4, TOK)
        kbT = cut(RQ, 4 * TOK, 4, TOK)
        vb = cut(RQ, 8 * TOK, TT, SBW)
        KR, VR = 4, 8
        kpg = cut(RQ, 8 * TOK + TT * SBW, KR, SBW)
        vpg = cut(RQ, 8 * TOK + TT * SBW + KR * SBW, VR, SBW)
        zb = cut(RX, 0, 3, 512)
        spb = cut(RX, 1536, 2, 512)
        Rp = cut(RX, 2560, 2, 512)
        Rs = cut(RX, 3584, 2, 5, 64)
        ab = cut(RX, 4224, 3, 512)
        ktp = cut(RX, 5760, 2, 512)
        mgT = cut(RQ, 0, KT, TOK)
        xn = cut(RQ, KT * TOK, 2, D)
        sg = cut(RQ, KT * TOK + 2 * D, 2, TOK)
        memT = cut(RQ, 0, KT, MEM)
        hmT = cut(RQ, 2048, KT, MEM)
        kmT = cut(RQ, 4096, 2, MEM)
        vmT = cut(RQ, 4608, 2, MEM)
        kvn = cut(RQ, 5120, 2, 2, GW)
        qcT = cut(RQ, 6144, 2, TOK)
        qcb = cut(RQ, 10752, 2, NB, 32)
        zeros = cut(RQ, 11264, MEM)
        pX = cut(RQ, 11520, 2, MEM)
        kvx = cut(RQ, 12032, 2, 512)
        ktx = cut(RQ, 13056, 2, 512)
        sqb = cut(RQ, 15616, 2, TOK)
        rb = cut(RQ, 17792, TOK)
        hid = cut(RQ, 0, 2, 4, TOK)
        yst = cut(RQ, 0, 2, D)
        ocT = oaT

        ident = sb("ident", [P, P])
        ones = sb("ones", [P, P])
        negones = sb("negones", [P, P])
        negtri = sb("negtri", [P, P])
        below = sb("below", [P, P])
        gains = sb("gains", [P, 5, KT])
        sbb = sb("sbb", [P, SBH])
        brow = sb("brow", [1, 4, 64])
        newmask = sb("newmask", [NEWK, NB, SBH, NQ])
        qbb = sb("qbb", [P, 4, NB, 16])
        mx = sb("mx", [P, len(sm), 3])
        nm = sb("nm", [P, len(sm)])
        Zs = sb("Zs", [P, len(sm)])
        rz = sb("rz", [P, len(sm)])
        pg = sb("pg", [1, NB * PAGES], I32)

        s_w = [sem(f"weights_landed{i}") for i in range(RING)]
        s_lin = sem("unit_in_psum")
        s_ea = sem("unit_emptied_by_scalar")
        s_ev = sem("unit_emptied_by_vector")
        s_dv = sem("vector_chain")
        s_aa = sem("scalar_chain")
        s_gp = sem("gpsimd_chain")
        s_cst = sem("constants_ready")
        s_small = sem("small_inputs_landed")
        s_x = [sem(f"x_tile_landed{i}") for i in range(2)]
        s_xt = sem("x_tile_turned")
        s_xe = sem("x_tile_in_sbuf")
        s_sq = sem("squares_ready")
        s_squ = sem("squares_used")
        s_var = sem("mean_square_ready")
        s_rt = sem("root_ready")
        s_h = sem("normed_ready")
        s_nt = sem("turned_pair_in_psum")
        s_nv = sem("turned_pair_in_sbuf")
        s_kout = [sem(f"k_rows_stored{i}") for i in range(2)]
        s_out = sem("stores_done")
        s_taps = sem("taps_ready")
        s_lines = sem("lines_stored")
        s_rep = sem("line_copies_stored")
        s_trow = sem("tap_rows_landed")
        s_T = [sem(f"bias_tile_landed{i}") for i in range(2)]
        s_ts = sem("sample_bias_ready")
        s_qk = sem("sample_queries_ready")
        s_kv = [sem(f"cache_chunk_landed{i}") for i in range(3)]
        s_ktm = sem("cache_keys_multiplied")
        s_vu = sem("cache_values_used")
        s_kx = [sem(f"memory_chunk_landed{i}") for i in range(2)]
        s_kt = sem("cache_keys_turned")
        s_ktv = sem("cache_keys_in_sbuf")
        s_S = sem("scores_ready")
        s_Sr = sem("scores_read")
        s_nmax = sem("negated_maximum_ready")
        s_p = sem("probabilities_ready")
        s_pn = sem("probabilities_scaled")
        s_pt = sem("probabilities_turned")
        s_pe = [sem("turned_probabilities_in_sbuf_by_vector"), sem("turned_probabilities_in_sbuf_by_scalar")]
        s_o = sem("attention_output_ready")
        s_oe = sem("attention_output_in_sbuf")
        s_ot = sem("attention_output_turned")
        s_ote = sem("attention_output_turned_in_sbuf")
        s_pg = sem("page_numbers_landed")
        s_kp = [sem(f"k_page_landed{i}") for i in range(KR)]
        s_vp = [sem(f"v_page_landed{i}") for i in range(VR)]
        s_bkt = sem("page_keys_turned")
        s_bktv = sem("page_keys_in_sbuf")
        s_bku = sem("page_keys_used")
        s_bS = sem("sb_scores_ready")
        s_bz = sem("sb_scores_clamped")
        s_bl = sem("sb_log_ready")
        s_bsp = sem("sb_softplus_ready")
        s_bR = sem("sb_running_sum_ready")
        s_bc = sem("sb_exponent_ready")
        s_ba = sem("sb_weights_ready")
        s_bam = sem("sb_weights_masked")
        s_bv = sem("sb_values_added")
        s_bo = sem("sb_output_in_sbuf")
        s_mg = sem("branches_merged")
        s_hs = sem("hidden_square_ready")
        s_yt = sem("y_tile_turned")
        s_ye = sem("y_tile_in_sbuf")
        s_yo = [sem(f"y_tile_stored{i}") for i in range(2)]

        def unit_emptied(eng, key):
            e, n = emptied[unit_no[key]]
            eng.wait_ge(s_ea if e == "a" else s_ev, n)

        slot_end = {}
        for name, n in (("qa", 3), ("ka", 3), ("va", 3), ("qb", 2), ("kb", 2), ("vb", 2), ("wo", 4), ("ck", 1), ("cv", 1),
                        ("cq", 1)):
            for s in range(n):
                slot_end[(name, s)] = unit_no[(name, 2 * s + 1)] + 1
        for s in range(4):
            slot_end[("ga", s)] = unit_no[("ga", 2 * s + 1)] + 1
            slot_end[("gb", s)] = unit_no[("gb", 2 * s + 1)] + 1
            slot_end[("br", s)] = unit_no[("bb", 2 * s + 1)] + 1
        slot_end[("co", 0)] = unit_no[("co", KT - 1)] + 1
        for c in range(NC):
            for s in range(2):
                slot_end[("up", c, s)] = unit_no[("up", c, 2 * s + 1)] + 1
                slot_end[("dn", c, s)] = unit_no[("dn", c, 4 * s + 3)] + 1
        slot_keys = sorted(slot_of, key=slot_of.get)
        w_count, total = [], [0] * RING
        for i, parts in enumerate(slots):
            total[i % RING] += 16 * len(parts)
            w_count.append(total[i % RING])

        turned = [(n, s) for n, c in (("ka", 3), ("va", 3), ("kb", 2), ("vb", 2)) for s in range(c)]
        turn_base = {k: 5 * i for i, k in enumerate(turned)}
        turn_base[("ck", 0)] = 5 * len(turned)
        turn_base[("cv", 0)] = 5 * len(turned) + 1
        k_slots = [k for k in turned if k[0][0] == "k"]

        wchunks = [("sw", hf, kv, b, part) for hf in range(2) for kv in range(2) for b in range(4) for part in range(3)]
        chunks = wchunks + [("sx", hf, kv, b, 0) for hf in range(2) for kv in range(2) for b in range(4)]
        chunk_no = {c: i for i, c in enumerate(chunks)}
        NWC = len(wchunks)

        def chunk_buf(n):
            return kvw[:, n % 3, :] if n < NWC else kvx[:, n % 2, :]

        def kv_wait(eng, n):
            if n < NWC:
                eng.wait_ge(s_kv[n % 3], 32 * (n // 3 + 1))
            else:
                eng.wait_ge(s_kx[n % 2], 16 * ((n - NWC) // 2 + 1))

        def chunk_tiles(c):
            if c[0] == "sx":
                return [(0, 0), (1, 1)]
            if c[4] == 0:
                return [(r, r) for r in range(5)]
            return [(r, 5 + 4 * (c[4] - 1) + r) for r in range(4)]

        turns, chunk_freed = [], {}
        values = 0
        for n, c in enumerate(chunks):
            if c[2] == 0:
                t = chunk_tiles(c)
                turns += [(n, t[i:i + 2]) for i in range(0, len(t), 2)]
                chunk_freed[n] = ("k", len(turns))
            else:
                values += 1
                chunk_freed[n] = ("v", values)

        def chunk_free(eng, n):
            kind, v = chunk_freed[n]
            eng.wait_ge(s_kt if kind == "k" else s_vu, v)

        outs_b = [i for i in range(NS) if i in last_of.values()]
        out_no = {i: n for n, i in enumerate(outs_b)}

        norm_order = [0, 3, 1, 2, 4]
        V_ROW_STORES = 2 * 5

        def p_of(u):
            kind = sm[u][0]
            return pS if kind == "sw" else pP[:, u % 2, :] if kind == "pw" else pX[:, u % 2, :]

        samples = [u for u, k in enumerate(sm) if k[0][0] == "s"]
        sample_no = {u: i for i, u in enumerate(samples)}

        def quad_evacuate(eng, copy, u, j):
            q = quad_base[u] + j
            if (q % 2 == 0) != (copy == nc.vector.tensor_copy):
                return
            eng.wait_ge(s_pt, q + 1)
            if u >= 1:
                eng.wait_ge(s_o, u)
            n = quads(u)[j][0][2]
            runs = [(x, w) for x, (_, _, w) in enumerate(quads(u)[j])]
            wide = [x for x, w in runs if w == P]
            thin = [x for x, w in runs if w < P]
            for xs, n in ((wide, P), (thin, NEWK)):
                if xs:
                    a, b = xs[0] * P, (xs[-1] + 1) * P
                    at = 512 * (4 + q % 2)
                    last = copy(PTs[0:n, j, a:b], psum[0:n, at + a:at + b])
            last.then_inc(s_pe[q % 2], 1)

        def needs_mask(s):
            return diagonal(s) or (s[0] == "s" and s[2] < 0)

        mask_no, n = {}, 0
        for i, s in enumerate(steps):
            if needs_mask(s):
                mask_no[i] = n
                n += 1

        def chain_of(s):
            return ("p", s[1], s[2]) if s[0] == "p" else ("s", s[1])

        before_of, place_of, seen = [], [], {}
        for i, s in enumerate(steps):
            c = chain_of(s)
            before_of.append(seen[c][0] if c in seen else None)
            place_of.append(seen[c][1] + 1 if c in seen else 0)
            seen[c] = (i, place_of[-1])

        def earlier(i):
            return before_of[i]

        def place(i):
            return place_of[i]

        def out_before(i):
            s = steps[i]
            if s[0] == "s":
                return out_no[last_of[("s", s[1] - 1)]] if s[1] else None
            return out_no[last_of[("p", s[1] - 1, s[2])]] if s[1] else None

        block = ctx.enter_context(nc.Block())

        @block.sync
        def _(sp):
            def weights(key):
                i = slot_of[key]
                if i >= RING:
                    sp.wait_ge(s_lin, slot_end[slot_keys[i - RING]])
                at = 0
                for src, k, n in slots[i]:
                    dst = ring[:, i % RING, at:at + k * n].rearrange("p (k n) -> p k n", k=k)
                    sp.dma_start(dst, src).then_inc(s_w[i % RING], 16)
                    at += k * n

            def x_tile(i):
                if i >= 2:
                    sp.wait_ge(s_xt, i - 1)
                t = i % TT
                if i < 2 * TT:
                    src = x_prompt[0, t * P:(t + 1) * P, :] if t < TT - 1 else x_sample.rearrange("b q d -> (b q) d")
                else:
                    t = i - 2 * TT
                    src = mem_prompt[0, t * P:(t + 1) * P, :]
                sp.dma_start(xn[0:src.shape[0], i % 2, :], src).then_inc(s_x[i % 2], 16)

            sp.dma_start(pg[:, :], page_table.rearrange("(o b) p -> o (b p)", o=1)).then_inc(s_pg, 16)
            for t in range(TT):
                x_tile(t)
                if t < RING:
                    weights(("qa", t))
            for name in ("ka", "va"):
                for s in range(3):
                    weights((name, s))
            sp.wait_ge(s_nv, turn_base[("va", 2)] + 5)
            sp.wait_ge(s_kout[0], 2 * 32)
            sp.wait_ge(s_kout[1], 32)
            for n, (_, hf, kv, b, part) in enumerate(wchunks):
                if n >= 3:
                    chunk_free(sp, n - 3)
                q = 4 * hf + b
                if part == 0:
                    sp.dma_start(kvw[:, n % 3, 0:GW],
                                 win_cache[kv][0, q].rearrange("k h d -> k (h d)")).then_inc(s_kv[n % 3], 16)
                    sp.dma_start(kvw[:, n % 3, GW:5 * GW],
                                 win_cache[2 + kv][0, q].rearrange("(p r) h d -> p (r h d)", r=4)).then_inc(s_kv[n % 3], 16)
                else:
                    r0 = 4 * (part - 1)
                    src = win_cache[4 + kv][0, q].rearrange("(p r) h d -> p r (h d)", r=16)[:, r0:r0 + 4, :]
                    sp.dma_start(kvw[:, n % 3, 0:4 * GW].rearrange("p (r f) -> p r f", r=4), src).then_inc(s_kv[n % 3], 32)
            sp.wait_ge(s_rep, 16 * 3 * HPG)
            sp.wait_ge(s_oe, 2)
            for h in range(HPG):
                if h >= 2:
                    sp.wait_ge(s_Sr, sm_no[("pw", h - 2, 7)] + 1)
                for g in range(3):
                    copy = line_copies[g * HPG + h]
                    src = bass.AP(tensor=copy.tensor, offset=copy.offset + P - 1,
                                  ap=[[max(LINE) - 1, P], [1, REACH[g] * P]])
                    sp.dma_start(Th[:, h % 2, SEG[g]:SEG[g + 1]], src).then_inc(s_T[h % 2], 16)
            for name in ("qb", "kb", "vb"):
                for s in range(2):
                    weights((name, s))
            sp.wait_ge(s_pg, 16)
            sp.wait_ge(s_ote, SEQ // P)
            sp.wait_ge(s_out, 16 * (len(win_cache) + 6))
            for n in range(NB * PAGES):
                i = (n // PAGES) * PAGES + PAGES - 1 - n % PAGES
                page = sp.value_load(pg[0:1, i:i + 1], min_val=0, max_val=sbk.shape[1] - 1)
                if n >= KR:
                    sp.wait_ge(s_bkt, n - KR + 1)
                sp.dma_start(kpg[:, n % KR, :],
                             sbk[0, bass.ds(page, 1)].rearrange("o t h d -> (o t) (h d)")).then_inc(s_kp[n % KR], 16)
                if n >= VR:
                    m = n - VR
                    sp.wait_ge(s_bv, steps.index(("s", m // PAGES, (m % PAGES) // 4)) + 1)
                sp.dma_start(vpg[:, n % VR, :],
                             sbv[0, bass.ds(page, 1)].rearrange("o t h d -> (o t) (h d)")).then_inc(s_vp[n % VR], 16)
            sp.wait_ge(s_bv, NS)
            sp.wait_ge(s_out, 16 * (len(win_cache) + V_ROW_STORES))
            for t in range(TT):
                x_tile(TT + t)
            for s in range(4):
                for name in ("ga", "gb", "br"):
                    weights((name, s))
            for s in range(4):
                weights(("wo", s))
            for t in range(2):
                x_tile(2 * TT + t)
            for name in ("ck", "cv", "cq"):
                weights((name, 0))
            unit_emptied(sp, ("wo", KT - 1))
            for n in range(NWC, len(chunks)):
                _, hf, kv, b, _ = chunks[n]
                if n >= NWC + 2:
                    chunk_free(sp, n - 2)
                sp.dma_start(chunk_buf(n),
                             (memk, memv)[kv][0, 4 * hf + b].rearrange("(p r) h d -> p (r h d)", r=2)).then_inc(s_kx[n % 2], 16)
            weights(("co", 0))
            for key in slot_keys:
                if key[0] in ("up", "dn"):
                    weights(key)

        @block.gpsimd
        def _(gp):
            chain = [0]

            def link(ins):
                chain[0] += 1
                ins.then_inc(s_gp, 1)
                gp.wait_ge(s_gp, chain[0])

            stored = [0]

            def store(dst, src):
                gp.dma_start(dst, src).then_inc(s_out, 16)
                stored[0] += 1

            with nc.allow_non_contiguous_dma(reason="small transposed inputs"):
                gp.dma_start(relT, rel_bias.rearrange("b h -> h b")).then_inc(s_small, 16)
                for i, g in enumerate((norm_mix, norm_cross, norm_mlp, norm_mem)):
                    gp.dma_start(gains[:, i, :], g[0].rearrange("(k p) -> p k", p=P)).then_inc(s_small, 16)
                gp.dma_start(gains[:, 4, :], norm_final.rearrange("(k p) -> p k", p=P)).then_inc(s_small, 16)
                gp.dma_start(sbb[:, :], sb_bias[0:1, :].to_broadcast([P, SBH])).then_inc(s_small, 16)
            link(nc.gpsimd.memset(ones[:, :], 1.0))
            link(nc.gpsimd.memset(negones[:, :], -1.0))
            link(nc.gpsimd.memset(ident[:, :], 0.0))
            link(nc.gpsimd.affine_select(out=ident[:, :], in_=ident[:, :], compare_op=ALU.not_equal, fill=1.0, base=0,
                                         pattern=[[-1, P]], channel_multiplier=1))
            link(nc.gpsimd.affine_select(out=negtri[:, :], in_=negones[:, :], compare_op=ALU.is_ge, fill=0.0, base=0,
                                         pattern=[[-1, P]], channel_multiplier=1))
            link(nc.gpsimd.affine_select(out=below[:, :], in_=ones[:, :], compare_op=ALU.is_gt, fill=0.0, base=0,
                                         pattern=[[1, P]], channel_multiplier=-1))

            def keep_new(t, b0, nb):
                link(nc.gpsimd.affine_select(out=t, in_=t, compare_op=ALU.is_ge, fill=0.0, base=-NQ * b0,
                                             pattern=[[-NQ, nb], [0, SBH], [0, NQ]], channel_multiplier=1))
                return nc.gpsimd.affine_select(out=t, in_=t, compare_op=ALU.is_gt, fill=0.0, base=NQ * b0,
                                               pattern=[[NQ, nb], [0, SBH], [1, NQ]], channel_multiplier=-1)

            link(nc.gpsimd.memset(newmask[:, :, :, :], 1.0))
            link(keep_new(newmask[:, :, :, :], 0, NB))
            link(nc.gpsimd.memset(ohw, 0.0))
            link(nc.gpsimd.affine_select(out=ohw, in_=ohw, compare_op=ALU.not_equal, fill=1.0, base=0,
                                         pattern=[[-8, 16], [-1, 8]], channel_multiplier=1))
            link(nc.gpsimd.memset(qblk, 0.0))
            nc.gpsimd.memset(qbb[:, :, :, :], 0.0).then_inc(s_cst, 1)

            for i, c in enumerate(win_cache):
                keep = c.shape[2]
                n = (keep - NQ) * GW
                store(s_win[i][0].rearrange("b k h d -> b (k h d)")[:, 0:n].rearrange("b (a c) -> b a c", a=8),
                      c[0].rearrange("b k h d -> b (k h d)")[:, NQ * GW:].rearrange("b (a c) -> b a c", a=8))

            gp.wait_ge(s_taps, 1)
            for g in range(3):
                at = LN + sum(LINE[:g])
                gp.dma_start(bias_lines[g * HPG:(g + 1) * HPG, 0:LINE[g]],
                             RQ[g * HPG:(g + 1) * HPG, at:at + LINE[g]]).then_inc(s_lines, 16)
            gp.wait_ge(s_lines, 16 * 3)
            for g in range(3):
                for h in range(HPG):
                    r = g * HPG + h
                    gp.dma_start(line_copies[r, :, 0:LINE[g]],
                                 bias_lines[r:r + 1, 0:LINE[g]].to_broadcast([P, LINE[g]])).then_inc(s_rep, 16)
            gp.dma_start(tap_rows.rearrange("h g m -> h (g m)"), taps.rearrange("p g m -> p (g m)")).then_inc(s_trow, 16)
            gp.wait_ge(s_trow, 16)
            for i in range(4):
                for h in range(HPG):
                    a = tap_rows[h:h + 1, 0:1, :]
                    src = bass.AP(tensor=a.tensor, offset=a.offset, ap=[[0, NQ], [(HPG * 3 + 1) * NTAPS, 3], [1, NTAPS]])
                    p0 = 32 * i + NQ * h
                    gp.dma_start(rowt[p0:p0 + NQ, :, :], src).then_inc(s_trow, 16)

            def rows_out(key, src, put):
                name, s = key
                if name in ("ka", "va"):
                    kv = 0 if name == "ka" else 1
                    dst, w = p_win[2 * s + kv], s_win[2 * s + kv]
                    t0 = TT - 1 - dst.shape[2] // P
                    put(dst[0, 0].rearrange("(t p) h d -> p t (h d)", p=P), src[:, t0:TT - 1, :])
                    n = w.shape[2]
                    put(w[0, :, n - NQ:n].rearrange("b j h d -> b j (h d)"), src[0:NEWK, TT - 1, :])
                else:
                    dst, w = (p_sbk, s_sbk) if name == "kb" else (p_sbv, s_sbv)
                    h0 = s * 4
                    put(dst[0, 0, :, h0:h0 + 4].rearrange("(t p) h d -> p t (h d)", p=P), src[:, 0:TT - 1, :])
                    put(w[0, :, :, h0:h0 + 4].rearrange("b j h d -> (b j) (h d)"), src[0:NEWK, TT - 1, :])

            for key in turned:
                gp.wait_ge(s_nv, turn_base[key] + 5)
                if key[0][0] == "k":
                    i = k_slots.index(key)
                    rows_out(key, kn[:, i % 2, :, :], lambda d, s: gp.dma_start(d, s).then_inc(s_kout[i % 2], 16))
                else:
                    src = va if key[0] == "va" else vb
                    rows_out(key, src[:, :, key[1] * GW:(key[1] + 1) * GW], store)
            masked = 0
            for i, s in enumerate(steps):
                if not needs_mask(s):
                    continue
                gp.wait_ge(s_ba, i + 1)
                if s[0] == "p":
                    t = ab[:, i % 3, lo_of(s):lo_of(s) + P]
                    nc.gpsimd.affine_select(out=t, in_=t, compare_op=ALU.is_gt, fill=0.0, base=0, pattern=[[1, P]],
                                            channel_multiplier=-1).then_inc(s_bam, 1)
                else:
                    t = ab[0:NEWK, i % 3, 0:64].rearrange("p (b h q) -> p b h q", b=1, h=SBH)
                    keep_new(t, s[1], 1).then_inc(s_bam, 1)
            for i, dst in enumerate((p_memk, p_memv)):
                gp.wait_ge(s_nv, 5 * len(turned) + i + 1)
                store(dst[0, 0].rearrange("(t p) h d -> p t (h d)", p=P), kvn[:, i, :, :])
            for t in range(TT):
                gp.wait_ge(s_ye, t + 1)
                n = P if t < TT - 1 else NEWK
                dst = y_p[0, t * P:(t + 1) * P, :] if t < TT - 1 else y_s.rearrange("b q d -> (b q) d")
                gp.dma_start(dst, yst[0:n, t % 2, :]).then_inc(s_yo[t % 2], 16)
            gp.wait_ge(s_yo[0], 16 * 5)
            gp.wait_ge(s_yo[1], 16 * 4)
            gp.wait_ge(s_out, 16 * stored[0])
            gp.wait_ge(s_kout[0], 3 * 32)
            gp.wait_ge(s_kout[1], 2 * 32)

        @block.tensor
        def _(pe):
            def set_of(u, n=TOK):
                at = 1536 * (u % 2)
                return psum[:, at:at + n]

            def free_set(u):
                if u >= 2:
                    e, n = emptied[u - 2]
                    pe.wait_ge(s_ea if e == "a" else s_ev, n)

            def unit(key, lhs, rhs, n=TOK):
                u = unit_no[key]
                free_set(u)
                out = set_of(u, n)
                for k, w in enumerate(lhs):
                    for c in range(0, n, 512):
                        e = min(c + 512, n)
                        last = pe.matmul(out[:, c:e], w, rhs[:, k, c:e], start=(k == 0), stop=(k == len(lhs) - 1))
                last.then_inc(s_lin, 1)

            def use_slot(key):
                i = slot_of[key]
                pe.wait_ge(s_w[i % RING], w_count[i])
                return ring[:, i % RING, :]

            def column_tile(view, k, n, c, at=0):
                w = view[:, at:at + k * n].rearrange("p (k n) -> p k n", k=k)
                return [w[:, j, c * P:(c + 1) * P] for j in range(k)]

            def norm(i, n=TOK):
                u = unit_no[("nm", i)]
                free_set(u)
                out = set_of(u, n)
                r = norm_order.index(i)
                for k in range(KT):
                    pe.wait_ge(s_sq, KT * r + k + 1)
                    for c in range(0, n, 512):
                        e = min(c + 512, n)
                        last = pe.matmul(out[:, c:e], ones[:, :], sqb[:, k % 2, c:e], start=(k == 0), stop=(k == KT - 1))
                    last.then_inc(s_squ if k < KT - 1 else s_lin, 1)
                pe.wait_ge(s_h, KT * (r + 1))

            def x_turn(i):
                pe.wait_ge(s_x[i % 2], 16 * (i // 2 + 1))
                if i >= 1:
                    pe.wait_ge(s_xe, i)
                n = NEWK if i in (TT - 1, 2 * TT - 1) else P
                for k in range(KT):
                    at = 3072 + k * P
                    last = pe.transpose(psum[:, at:at + n], xn[0:n, i % 2, k * P:(k + 1) * P], ident[0:n, 0:n])
                last.then_inc(s_xt, 1)

            def turn_rows(key):
                name, s = key
                for c in range(2):
                    unit_emptied(pe, (name, 2 * s + c))
                for j in range(5 if name[0] != "c" else 1):
                    i = turn_base[key] + j
                    if i >= 2:
                        pe.wait_ge(s_nv, i - 1)
                    for t in range(2 * j, min(2 * j + 2, TT)):
                        n = P if t < TT - 1 else NEWK
                        for c in range(2):
                            src = {"ka": kaT, "kb": kbT, "ck": kmT}.get(name)
                            src = src[:, 2 * s + c, :] if src is not None else (vmT if name == "cv" else vt)[:, c, :]
                            o = 512 * (6 + i % 2) + (t - 2 * j) * GW + c * P
                            last = pe.transpose(psum[0:n, o:o + P], src[:, t * P:t * P + n], ident[:, :])
                    last.then_inc(s_nt, 1)

            def project(names):
                before = None
                for name, n in names:
                    for s in range(n):
                        v = use_slot((name, s))
                        for c in range(2):
                            unit((name, 2 * s + c), column_tile(v, KT, SLOTW, c), hT)
                        if before:
                            turn_rows(before)
                        before = (name, s) if name[0] != "q" else None
                turn_rows(before)

            def prompt_scores(u):
                kind, h, t = sm[u]
                if u >= 1:
                    pe.wait_ge(s_Sr, u)
                hp = HD * (h % 2)
                runs, col = [], 0
                for g, b, w in blocks(u):
                    if runs and runs[-1][0] == g and col % 512:
                        runs[-1][3] += w
                    else:
                        runs.append([g, b, col, w])
                    col += w
                for g, b, col, w in runs:
                    q, k = (qaT, kaT) if kind == "pw" else (qcT, kmT)
                    j = 2 * g + h // 2
                    last = pe.matmul(psum[:, col:col + w], q[hp:hp + HD, j, t * P:(t + 1) * P],
                                     k[hp:hp + HD, j, b * P:b * P + w], start=True, stop=True)
                last.then_inc(s_S, 1)

            def sample_scores(u):
                kind, hf = sm[u]
                if u >= 1:
                    pe.wait_ge(s_Sr, u)
                    pe.wait_ge(s_oe, u)
                mine = [i for i, (n, _) in enumerate(turns) if chunks[n][0:2] == (kind, hf)]
                qs = qblk if kind == "sw" else qcb
                kts = ktw if kind == "sw" else ktx

                def multiply(i):
                    n, tiles = turns[i]
                    b = chunks[n][3]
                    pe.wait_ge(s_ktv, i + 1)
                    for x, (_, blk) in enumerate(tiles):
                        g = blocks(u)[blk][0]
                        for pair in range(2):
                            last = pe.matmul(psum[32 * b:32 * b + 32, blk * P:(blk + 1) * P],
                                             qs[:, 2 * g + pair, 4 * hf + b, :],
                                             kts[:, i % 2, (2 * x + pair) * P:(2 * x + pair + 1) * P],
                                             start=(pair == 0), stop=(pair == 1))
                    if kind == "sw" and i + 1 < len(turns) and turns[i + 1][0] != n and chunks[n][4] == 2:
                        for g in range(3):
                            for pair in range(2):
                                at = OLDK + g * NEWK
                                last = pe.matmul(psum[32 * b:32 * b + 32, at:at + NEWK], qs[:, 2 * g + pair, 4 * hf + b, :],
                                                 kaT[:, 2 * g + pair, SEQ:TOK], start=(pair == 0), stop=(pair == 1))
                    last.then_inc(s_ktm, 1)

                for i in mine:
                    n, tiles = turns[i]
                    kv_wait(pe, n)
                    if i >= 2:
                        pe.wait_ge(s_ktv, i - 1)
                    for x, (r, _) in enumerate(tiles):
                        for pair in range(2):
                            at = 512 * (6 + i % 2) + (2 * x + pair) * P
                            last = pe.transpose(psum[:, at:at + P],
                                                chunk_buf(n)[:, r * GW + pair * P:r * GW + (pair + 1) * P], ident[:, :])
                    last.then_inc(s_kt, 1)
                    if i > mine[0]:
                        multiply(i - 1)
                multiply(mine[-1])
                pe.drain().then_inc(s_S, 1)

            def turn_quad(u, j):
                q = quad_base[u] + j
                if q >= 2:
                    pe.wait_ge(s_pe[q % 2], q // 2)
                for x, (_, _, w) in enumerate(quads(u)[j]):
                    col = sum(b[2] for b in blocks(u)[0:4 * j + x])
                    at = 512 * (4 + q % 2) + x * P
                    last = pe.transpose(psum[0:w, at:at + P], p_of(u)[:, col:col + w], ident[:, :])
                last.then_inc(s_pt, 1)

            def prompt_values(u):
                kind, h, t = sm[u]
                pe.wait_ge(s_p, u + 1)
                n = len(quads(u))
                o = psum[:, 512 * (6 + u % 2):512 * (6 + u % 2) + HD]

                def multiply(j):
                    q = quad_base[u] + j
                    pe.wait_ge(s_pe[q % 2], q // 2 + 1)
                    if j == 0 and u >= 2:
                        pe.wait_ge(s_oe, u - 1)
                    for x, (g, b, _) in enumerate(quads(u)[j]):
                        v = va[:, b, g * GW + h * HD:g * GW + (h + 1) * HD] if kind == "pw" else kvn[:, 1, b, h * HD:(h + 1) * HD]
                        last = pe.matmul(o, PTs[:, j, x * P:(x + 1) * P], v, start=(4 * j + x == 0),
                                         stop=(4 * j + x == len(blocks(u)) - 1))
                    return last

                for j in range(n):
                    turn_quad(u, j)
                    if j >= 1:
                        multiply(j - 1)
                multiply(n - 1).then_inc(s_o, 1)

            def sample_values(u):
                kind, hf = sm[u]
                pe.wait_ge(s_pn, sample_no[u] + 1)
                for j in range(len(quads(u))):
                    turn_quad(u, j)
                for j in range(max(0, len(quads(u)) - 2), len(quads(u))):
                    q = quad_base[u] + j
                    pe.wait_ge(s_pe[q % 2], q // 2 + 1)
                if u >= 2:
                    pe.wait_ge(s_oe, u - 1)
                pe.wait_ge(s_ktv, max(i for i, (n, _) in enumerate(turns) if chunks[n][0:2] == (kind, hf)) + 1)
                first = True
                for b in range(4):
                    for part in range(3 if kind == "sw" else 1):
                        n = chunk_no[(kind, hf, 1, b, part)]
                        kv_wait(pe, n)
                        tiles = [(chunk_buf(n)[:, r * GW:(r + 1) * GW], blk) for r, blk in chunk_tiles(chunks[n])]
                        if kind == "sw" and part == 2:
                            tiles = [(va[0:NEWK, TT - 1, g * GW:(g + 1) * GW], 13 + g) for g in range(3)] + tiles
                        for v, blk in tiles:
                            w = blocks(u)[blk][2]
                            for pair in range(2):
                                at = 512 * (6 + u % 2) + (2 * b + pair) * 16
                                pt = PTs[0:w, blk // 4, (blk % 4) * P + 32 * b + 16 * pair:(blk % 4) * P + 32 * b + 16 * pair + 16]
                                last = pe.matmul(psum[:, at:at + 16], v[:, pair * P:(pair + 1) * P], pt, start=first,
                                                 stop=(blk == tiles[-1][1] and part == (2 if kind == "sw" else 0)),
                                                 skip_group_check=True)
                                first = False
                        last.then_inc(s_vu, 1)
                pe.drain().then_inc(s_o, 1)

            def attend(kinds):
                mine = [u for u, k in enumerate(sm) if k[0] in kinds]
                for u in mine:
                    if sm[u][0][0] == "s":
                        sample_scores(u)
                        sample_values(u)
                        continue
                    prompt_scores(u)
                    if sm[u - 1][0][0] == "p":
                        prompt_values(u - 1)
                prompt_values(mine[-1])

            def turn_outputs(first_oe, n0):
                pe.wait_ge(s_oe, first_oe)
                for e in range(2):
                    m = (quad_base[first_oe] - 1 - e)
                    pe.wait_ge(s_pe[m % 2], m // 2 + 1)
                for t in range(SEQ // P):
                    if t >= 2:
                        pe.wait_ge(s_ote, n0 + t - 1)
                    for c in range(2):
                        at = 512 * (4 + t % 2) + c * P
                        last = pe.transpose(psum[:, at:at + P], onat[:, t, c * P:(c + 1) * P], ident[:, :])
                    last.then_inc(s_ot, 1)

            def sb_scores(i):
                s = steps[i]
                if i >= 3:
                    pe.wait_ge(s_ba, i - 2)
                out = bank(i % 3)
                if s[0] == "p":
                    _, h, c, b = s
                    hp, lo = HD * (h % 2), lo_of(s)
                    pe.matmul(out[:, lo:512], kbT[hp:hp + HD, h // 2, b * P:(b + 1) * P],
                              qbT[hp:hp + HD, h // 2, c * 512 + lo:(c + 1) * 512], start=True, stop=True).then_inc(s_bS, 1)
                    return
                _, b, g = s
                n = rows(s)
                w = span(s)
                pe.matmul(out[0:n, 0:w], ones[0:1, 0:n], brow[0:1, :, :].rearrange("o j n -> o (j n)")[:, 0:w],
                          start=True, stop=False, skip_group_check=True)
                if g < 0:
                    for pair in range(4):
                        last = pe.matmul(out[0:n, pair * 16:(pair + 1) * 16], kbT[:, pair, SEQ:TOK], qbb[:, pair, b, :],
                                         start=False, stop=(pair == 3), skip_group_check=True)
                    last.then_inc(s_bS, 1)
                    return

                def page_scores(x):
                    n = b * PAGES + 4 * g + x
                    pe.wait_ge(s_bktv, n + 1)
                    for pair in range(4):
                        at = (3 - x) * 64 + pair * 16
                        last = pe.matmul(out[:, at:at + 16], ktp[:, n % 2, pair * P:(pair + 1) * P], qbb[:, pair, b, :],
                                         start=False, stop=(x == 3), skip_group_check=True)
                    last.then_inc(s_bku if x < 3 else s_bS, 1)

                for x in range(4):
                    n = b * PAGES + 4 * g + x
                    pe.wait_ge(s_kp[n % KR], 16 * (n // KR + 1))
                    if n >= 2:
                        pe.wait_ge(s_bktv, n - 1)
                    for pair in range(4):
                        at = 512 * (6 + n % 2) + pair * P
                        last = pe.transpose(psum[:, at:at + P], kpg[:, n % KR, pair * P:(pair + 1) * P], ident[:, :])
                    last.then_inc(s_bkt, 1)
                    if x >= 1:
                        page_scores(x - 1)
                page_scores(3)

            def sb_exponent(i):
                s = steps[i]
                n = rows(s)
                lo = lo_of(s) if s[0] == "p" else 0
                hi = lo + span(s)
                out = bank(i % 3)[0:n, lo:hi]
                before = earlier(i)
                pe.wait_ge(s_bsp, i + 1)
                last = pe.matmul(out, negtri[0:n, 0:n], spb[0:n, i % 2, lo:hi], start=False, stop=before is None,
                                 skip_group_check=True)
                if before is not None:
                    if s[0] == "p":
                        pe.wait_ge(s_bR, before + 1)
                        r = Rp[:, place(i) % 2, lo:hi]
                    else:
                        pe.wait_ge(s_bR, i + 1)
                        r = Rs[:, s[2] % 2, 1:5, :].rearrange("p j n -> p (j n)")
                    last = pe.matmul(out, negones[:, :], r, start=False, stop=True, skip_group_check=True)
                last.then_inc(s_bc, 1)

            def sb_values(i):
                s = steps[i]
                pe.wait_ge(s_ba, i + 1)
                if needs_mask(s):
                    pe.wait_ge(s_bam, mask_no[i] + 1)
                first = earlier(i) is None
                if s[0] == "p":
                    _, h, c, b = s
                    hp, lo = HD * (h % 2), lo_of(s)
                    if first and out_before(i) is not None:
                        pe.wait_ge(s_bo, out_before(i) + 1)
                    o = bank(3 + 2 * c)[hp:hp + HD, lo:512]
                    pe.matmul(o, vb[:, b, h * HD:(h + 1) * HD], ab[:, i % 3, lo:512], start=first, stop=(b == 0),
                              skip_group_check=True).then_inc(s_bv, 1)
                    return
                _, b, g = s
                if first and out_before(i) is not None:
                    pe.wait_ge(s_bo, out_before(i) + 1)
                for x in range(4 if g >= 0 else 1):
                    n = b * PAGES + 4 * g + x
                    if g >= 0:
                        pe.wait_ge(s_vp[n % VR], 16 * (n // VR + 1))
                    for pair in range(4):
                        at = 16 * pair
                        if g < 0:
                            v, a = vb[0:NEWK, TT - 1, pair * P:(pair + 1) * P], ab[0:NEWK, i % 3, at:at + 16]
                        else:
                            v = vpg[:, n % VR, pair * P:(pair + 1) * P]
                            a = ab[:, i % 3, (3 - x) * 64 + at:(3 - x) * 64 + at + 16]
                        last = pe.matmul(bank(4)[:, at:at + 16], v, a, start=(g < 0 and pair == 0), stop=(g == 3 and x == 3),
                                         skip_group_check=True)
                last.then_inc(s_bv, 1)

            pe.wait_ge(s_cst, 1)
            for t in range(TT):
                x_turn(t)
            norm(0)
            project((("qa", 3), ("ka", 3), ("va", 3)))
            pe.wait_ge(s_qk, 1)
            unit_emptied(pe, ("va", 4))
            unit_emptied(pe, ("va", 5))
            pe.wait_ge(s_nv, turn_base[("va", 2)] + 5)
            attend(("sw", "pw"))
            turn_outputs(sm_no[("pw", HPG - 1, 7)] + 1, 0)
            pe.wait_ge(s_Sr, sm_no[("pw", HPG - 1, 7)] + 1)
            pe.wait_ge(s_ote, SEQ // P)
            project((("qb", 2), ("kb", 2), ("vb", 2)))
            pe.wait_ge(s_qk, 2)
            unit_emptied(pe, ("vb", 2))
            unit_emptied(pe, ("vb", 3))
            pe.wait_ge(s_nv, turn_base[("vb", 1)] + 5)
            for i in range(NS + 2):
                if i < NS:
                    sb_scores(i)
                if i >= 2:
                    sb_values(i - 2)
                if 1 <= i <= NS:
                    sb_exponent(i - 1)
            pe.wait_ge(s_bo, len(outs_b))
            pe.wait_ge(s_ba, NS)
            for t in range(TT):
                x_turn(TT + t)
            for s in range(4):
                wa = use_slot(("ga", s))
                wb = use_slot(("gb", s))
                wr = use_slot(("br", s))
                for c in range(2):
                    i = 2 * s + c
                    unit(("ga", i), column_tile(wa, KT, SLOTW, c), hT)
                    unit(("ba", i), column_tile(wr, 2, SLOTW, c), oaT)
                    unit(("gb", i), column_tile(wb, KT, SLOTW, c), hT)
                    unit(("bb", i), column_tile(wr, 4, SLOTW, c, 2 * SLOTW), obT)
            pe.wait_ge(s_mg, KT)
            for i in range(KT):
                unit(("wo", i), column_tile(use_slot(("wo", i // 2)), KT, SLOTW, i % 2), mgT)
            for t in range(2):
                x_turn(2 * TT + t)
            norm(3, MEM)
            for name in ("ck", "cv"):
                for i in range(2):
                    unit((name, i), column_tile(use_slot((name, 0)), KT, SLOTW, i), hmT, MEM)
            turn_rows(("ck", 0))
            turn_rows(("cv", 0))
            norm(1)
            for i in range(2):
                unit(("cq", i), column_tile(use_slot(("cq", 0)), KT, SLOTW, i), hT)
            pe.wait_ge(s_qk, 3)
            unit_emptied(pe, ("cq", 0))
            unit_emptied(pe, ("cq", 1))
            pe.wait_ge(s_nv, 5 * len(turned) + 2)
            attend(("sx", "px"))
            turn_outputs(len(sm), SEQ // P)
            pe.wait_ge(s_ote, 2 * (SEQ // P))
            for i in range(KT):
                unit(("co", i), column_tile(use_slot(("co", 0)), 2, D, i), oaT)
            norm(2)
            for c in range(NC + 1):
                if c < NC:
                    for i in range(4):
                        unit(("up", c, i), column_tile(use_slot(("up", c, i // 2)), KT, SLOTW, i % 2), hT)
                if c >= 1:
                    pe.wait_ge(s_hs, 4 * c)
                    for i in range(KT):
                        unit(("dn", c - 1, i), column_tile(use_slot(("dn", c - 1, i // 4)), 4, 512, i % 4), hid[:, (c - 1) % 2, :, :])
            norm(4)
            for t in range(TT):
                if t >= 1:
                    pe.wait_ge(s_ye, t)
                n = P if t < TT - 1 else NEWK
                for k in range(KT):
                    last = pe.transpose(psum[0:n, 3072 + k * P:3072 + (k + 1) * P], hT[:, k, t * P:t * P + n], ident[:, :])
                last.then_inc(s_yt, 1)

        @block.scalar
        def _(act):
            chain = [0]

            def link(ins):
                chain[0] += 1
                ins.then_inc(s_aa, 1)
                act.wait_ge(s_aa, chain[0])

            def take(key, n=TOK):
                u = unit_no[key]
                act.wait_ge(s_lin, u + 1)
                at = 1536 * (u % 2)
                return psum[:, at:at + n]

            def x_evacuate(i):
                act.wait_ge(s_xt, i + 1)
                n = NEWK if i in (TT - 1, 2 * TT - 1) else P
                t = i % TT if i < 2 * TT else i - 2 * TT
                dst = (xT if i < 2 * TT else memT)[:, :, t * P:t * P + n]
                nc.scalar.copy(dst, psum[:, 3072:4096].rearrange("p (k n) -> p k n", k=KT)[:, :, 0:n]).then_inc(s_xe, 1)

            def norm(i, src, n=TOK):
                r = norm_order.index(i)
                for k in range(KT):
                    if k >= 2:
                        act.wait_ge(s_squ, (KT - 1) * r + k - 1)
                    nc.scalar.activation(sqb[:, k % 2, 0:n], src[:, k, 0:n], ACT.Square).then_inc(s_sq, 1)
                act.wait_ge(s_var, r + 1)
                nc.scalar.activation(rb[:, 0:n], rb[:, 0:n], ACT.Sqrt).then_inc(s_rt, 1)

            def project(names):
                for name, n in names:
                    for i in range(2 * n):
                        if name[0] == "v" and i % 2 == 0:
                            if (name, i // 2) != ("va", 0):
                                k = (name, i // 2 - 1) if i else ("va", 2)
                                act.wait_ge(s_nt, turn_base[k] + 5)
                        ps = take((name, i))
                        if name[0] == "q":
                            dst = (qaT if name == "qa" else qbT)[:, i, :]
                            nc.scalar.mul(dst, ps, HD ** -0.5).then_inc(s_ea, 1)
                        else:
                            dst = (kaT if name == "ka" else kbT)[:, i, :] if name[0] == "k" else vt[:, i % 2, :]
                            nc.scalar.copy(dst, ps).then_inc(s_ea, 1)

            def turned_keys(i):
                n, tiles = turns[i]
                kts = ktw if n < NWC else ktx
                act.wait_ge(s_kt, i + 1)
                if i >= 2:
                    act.wait_ge(s_ktm, i - 1)
                w = 2 * P * len(tiles)
                at = 512 * (6 + i % 2)
                nc.scalar.copy(kts[:, i % 2, 0:w], psum[:, at:at + w]).then_inc(s_ktv, 1)

            def probabilities(u):
                act.wait_ge(s_nmax, u + 1)
                w = width(u)
                nc.scalar.activation(p_of(u)[:, 0:w], p_of(u)[:, 0:w], ACT.Exp, bias=nm[:, u:u + 1],
                                     accum_out=Zs[:, u:u + 1]).then_inc(s_p, 1)

            def quad_out(u, j):
                quad_evacuate(act, nc.scalar.copy, u, j)

            def attend(kinds):
                mine = [u for u, k in enumerate(sm) if k[0] in kinds]
                for u in mine:
                    if sm[u][0][0] == "s":
                        for i, (n, _) in enumerate(turns):
                            if chunks[n][0:2] == sm[u]:
                                turned_keys(i)
                    probabilities(u)
                    if sm[u][0][0] == "s":
                        for j in range(len(quads(u))):
                            quad_out(u, j)
                    elif sm[u - 1][0][0] == "p":
                        for j in range(len(quads(u - 1))):
                            quad_out(u - 1, j)
                for j in range(len(quads(mine[-1]))):
                    quad_out(mine[-1], j)

            for t in range(TT):
                x_evacuate(t)
            act.wait_ge(s_xe, TT)
            norm(0, xT)
            project((("qa", 3),))
            act.wait_ge(s_ts, 1)
            act.wait_ge(s_lines, 16 * 3)
            project((("ka", 3), ("va", 3)))
            attend(("sw", "pw"))
            project((("qb", 2), ("kb", 2), ("vb", 2)))

            def page_keys(n):
                act.wait_ge(s_bkt, n + 1)
                if n >= 2:
                    m = n - 2
                    if m % 4 < 3:
                        act.wait_ge(s_bku, 3 * (m // 4) + m % 4 + 1)
                    else:
                        act.wait_ge(s_bS, steps.index(("s", m // PAGES, (m % PAGES) // 4)) + 1)
                at = 512 * (6 + n % 2)
                nc.scalar.copy(ktp[:, n % 2, :], psum[:, at:at + 512]).then_inc(s_bktv, 1)

            for i in range(NS + 1):
                if i < NS:
                    s = steps[i]
                    n, w = rows(s), span(s)
                    lo = lo_of(s) if s[0] == "p" else 0
                    if s[0] == "s" and s[2] >= 0:
                        for x in range(4):
                            page_keys(s[1] * PAGES + 4 * s[2] + x)
                    z = zb[0:n, i % 3, lo:lo + w]
                    act.wait_ge(s_bz, i + 1)
                    link(nc.scalar.activation(z, z, ACT.Exp))
                    nc.scalar.activation(z, z, ACT.Ln, bias=1.0).then_inc(s_bl, 1)
                if i >= 1:
                    s = steps[i - 1]
                    n, w = rows(s), span(s)
                    lo = lo_of(s) if s[0] == "p" else 0
                    act.wait_ge(s_bc, i)
                    if i - 1 >= 3:
                        act.wait_ge(s_bv, i - 3)
                    bias = sbb[:, s[1]:s[1] + 1] if s[0] == "p" else 0.0
                    nc.scalar.activation(ab[0:n, (i - 1) % 3, lo:lo + w], bank((i - 1) % 3)[0:n, lo:lo + w], ACT.Exp,
                                         bias=bias).then_inc(s_ba, 1)
            act.wait_ge(s_bv, NS)
            act.wait_ge(s_bR, NS)
            for t in range(TT):
                x_evacuate(TT + t)
            for i in range(KT):
                for j, (g, b) in enumerate((("ga", "ba"), ("gb", "bb"))):
                    ps = take((g, i))
                    if i:
                        unit_emptied(act, (b, i - 1))
                        if j:
                            act.wait_ge(s_mg, i)
                    nc.scalar.activation(sg[:, j, :], ps, ACT.Sigmoid).then_inc(s_ea, 1)
            act.wait_ge(s_lin, unit_no[("wo", KT - 1)] + 1)
            for t in range(2):
                x_evacuate(2 * TT + t)
            act.wait_ge(s_xe, 2 * TT + 2)
            norm(3, memT, MEM)
            for name, dst in (("ck", kmT), ("cv", vmT)):
                for i in range(2):
                    nc.scalar.copy(dst[:, i, :], take((name, i), MEM)).then_inc(s_ea, 1)
            unit_emptied(act, ("wo", KT - 1))
            norm(1, xT)
            for i in range(2):
                nc.scalar.mul(qcT[:, i, :], take(("cq", i)), HD ** -0.5).then_inc(s_ea, 1)
            attend(("sx", "px"))
            unit_emptied(act, ("co", KT - 1))
            norm(2, xT)
            act.wait_ge(s_out, 16 * (len(win_cache) + V_ROW_STORES + 2))
            for c in range(NC):
                if c >= 2:
                    act.wait_ge(s_lin, unit_no[("dn", c - 2, KT - 1)] + 1)
                for i in range(4):
                    nc.scalar.activation(hid[:, c % 2, i, :], take(("up", c, i)), ACT.Relu).then_inc(s_ea, 1)
            unit_emptied(act, ("dn", NC - 1, KT - 1))
            norm(4, xT)
            for t in range(TT):
                act.wait_ge(s_yt, t + 1)
                if t >= 2:
                    act.wait_ge(s_yo[t % 2], 16 * (t // 2))
                n = P if t < TT - 1 else NEWK
                nc.scalar.copy(yst[0:n, t % 2, :], psum[0:n, 3072:4096]).then_inc(s_ye, 1)

        @block.vector
        def _(dve):
            chain = [0]

            def link(ins):
                chain[0] += 1
                ins.then_inc(s_dv, 1)
                dve.wait_ge(s_dv, chain[0])

            def take(key, n=TOK):
                u = unit_no[key]
                dve.wait_ge(s_lin, u + 1)
                at = 1536 * (u % 2)
                return psum[:, at:at + n]

            def norm(i, gain, src, dst, n=TOK):
                r = norm_order.index(i)
                nc.vector.tensor_scalar(rb[:, 0:n], take(("nm", i), n), 1.0 / D, EPS, ALU.mult, ALU.add).then_inc(s_ev, 1)
                unit_emptied(dve, ("nm", i))
                nc.vector.reciprocal(rb[:, 0:n], rb[:, 0:n]).then_inc(s_var, 1)
                dve.wait_ge(s_rt, r + 1)
                for k in range(KT):
                    nc.vector.scalar_tensor_tensor(out=dst[:, k, 0:n], in0=src[:, k, 0:n], scalar=gains[:, gain, k:k + 1],
                                                   in1=rb[:, 0:n], op0=ALU.mult, op1=ALU.mult).then_inc(s_h, 1)

            def rows_in(key):
                name, s = key
                if name[0] == "k":
                    i = k_slots.index(key)
                    if i >= 2:
                        dve.wait_ge(s_kout[i % 2], 32 * (i // 2))
                    dst = kn[:, i % 2, :, :]
                elif name[0] == "v":
                    dst = (va if name == "va" else vb)[:, :, s * GW:(s + 1) * GW]
                else:
                    dst = kvn[:, 0 if name == "ck" else 1, :, :]
                for j in range(5 if name[0] != "c" else 1):
                    i = turn_base[key] + j
                    dve.wait_ge(s_nt, i + 1)
                    n, m = (P, 2) if 2 * j < TT - 1 else (NEWK, 1)
                    at = 512 * (6 + i % 2)
                    nc.vector.tensor_copy(dst[0:n, 2 * j:2 * j + m, :],
                                          psum[0:n, at:at + m * GW].rearrange("p (t n) -> p t n", t=m)).then_inc(s_nv, 1)

            def block_queries(src, dst, groups):
                for j in range(2 * groups):
                    for e in range(2):
                        c = (2 * (j % 2) + e) * NQ
                        last = nc.vector.tensor_copy(
                            dst[HD * e:HD * (e + 1), j, :, c:c + NQ],
                            src[HD * e:HD * (e + 1), j, SEQ:TOK].rearrange("p (b q) -> p b q", b=NB))
                last.then_inc(s_qk, 1)

            def scores(u):
                kind = sm[u][0]
                if kind[0] == "p":
                    if u >= 2:
                        dve.wait_ge(s_pt, quad_base[u - 1])
                else:
                    dve.wait_ge(s_pt, quad_base[u]) if quad_base[u] else None
                dve.wait_ge(s_S, u + 1)
                p = p_of(u)
                if kind == "sw":
                    hf = sm[u][1]
                    parts = [(0, OLDK, Ts), (OLDK, WINW, TsN[:, hf, :, :].rearrange("p g n -> p (g n)"))]
                elif kind == "pw":
                    h = sm[u][1]
                    dve.wait_ge(s_T[h % 2], 48 * (h // 2 + 1))
                    parts, at = [], 0
                    for g in range(3):
                        n = min(REACH[g], sm[u][2] + 1) * P
                        parts.append((at, at + n, Th[:, h % 2, SEG[g + 1] - n:SEG[g + 1]]))
                        at += n
                else:
                    parts = [(0, MEM, zeros)]
                for x, (a, b, t) in enumerate(parts):
                    last = nc.vector.tensor_tensor_reduce(out=p[:, a:b], in0=psum[:, a:b], in1=t, scale=1.0, scalar=LOW,
                                                          op0=ALU.add, op1=ALU.max, accum_out=mx[:, u, x:x + 1])
                last.then_inc(s_Sr, 1)
                dve.wait_ge(s_Sr, u + 1)
                link(nc.vector.tensor_reduce(nm[:, u:u + 1], mx[:, u, 0:len(parts)], AX.X, ALU.max))
                nc.vector.tensor_scalar(nm[:, u:u + 1], nm[:, u:u + 1], -1.0, None, ALU.mult).then_inc(s_nmax, 1)

            def quad_out(u, j):
                quad_evacuate(dve, nc.vector.tensor_copy, u, j)

            def reciprocal(u):
                dve.wait_ge(s_p, u + 1)
                link(nc.vector.reciprocal(rz[:, u:u + 1], Zs[:, u:u + 1]))

            def sample_unit(u):
                scores(u)
                reciprocal(u)
                w = width(u)
                p = p_of(u)[:, 0:w]
                nc.vector.tensor_scalar(p, p, rz[:, u:u + 1], None, ALU.mult).then_inc(s_pn, 1)
                for j in range(len(quads(u))):
                    quad_out(u, j)
                dve.wait_ge(s_o, u + 1)
                hf = sm[u][1]
                o = psum[:, 512 * (6 + u % 2):512 * (6 + u % 2) + P].rearrange("p (b j n) -> p j b n", b=4, j=2)
                for e in range(2):
                    for j in range(2):
                        last = nc.vector.tensor_copy(
                            oaT[HD * e:HD * (e + 1), j, SEQ + 32 * hf:SEQ + 32 * (hf + 1)].rearrange("p (b q) -> p b q", b=4),
                            o[HD * e:HD * (e + 1), j, :, NQ * e:NQ * (e + 1)])
                last.then_inc(s_oe, 1)

            def prompt_output(u):
                _, h, t = sm[u]
                for j in range(len(quads(u))):
                    quad_out(u, j)
                reciprocal(u)
                dve.wait_ge(s_o, u + 1)
                at = 512 * (6 + u % 2)
                nc.vector.tensor_scalar(onat[:, t, h * HD:(h + 1) * HD], psum[:, at:at + HD], rz[:, u:u + 1], None,
                                        ALU.mult).then_inc(s_oe, 1)

            def attend(kinds, n0):
                mine = [u for u, k in enumerate(sm) if k[0] in kinds]
                for u in mine:
                    if sm[u][0][0] == "s":
                        sample_unit(u)
                        continue
                    scores(u)
                    if sm[u - 1][0][0] == "p":
                        prompt_output(u - 1)
                prompt_output(mine[-1])
                for t in range(SEQ // P):
                    dve.wait_ge(s_ot, n0 + t + 1)
                    at = 512 * (4 + t % 2)
                    nc.vector.tensor_copy(oaT[:, :, t * P:(t + 1) * P],
                                          psum[:, at:at + 2 * P].rearrange("p (c n) -> p c n", c=2)).then_inc(s_ote, 1)

            dve.wait_ge(s_small, 16 * 7)
            link(nc.vector.memset(lines, NEG))
            for g, (_, d) in enumerate(GROUPS):
                for m0, m1, b in bucket_runs(d):
                    i0, i1 = NTAPS - m1, NTAPS - m0
                    last = nc.vector.tensor_copy(taps[:, g, i0:i1], relT[:, b:b + 1].to_broadcast([12, i1 - i0]))
            link(last)
            for g, (_, d) in enumerate(GROUPS):
                n = REACH[g] * P
                far = min(NTAPS - 1, (n - 1) // d)
                z0 = sum(LINE[:g]) + n - 1 - d * far
                last = nc.vector.tensor_copy(lines[:, z0:z0 + d * far + 1:d], taps[:, g, NTAPS - 1 - far:NTAPS])
            last.then_inc(s_taps, 1)
            for j in range(4):
                last = nc.vector.tensor_copy(brow[:, j, :].rearrange("o (h q) -> o h q", h=SBH),
                                             sbb[0:1, :].rearrange("o (h u) -> o h u", u=1).to_broadcast([1, SBH, NQ]))
            dve.wait_ge(s_cst, 1)
            link(nc.vector.tensor_reduce(oh, ohw.rearrange("p i r -> p r i"), AX.X, ALU.add))
            link(nc.vector.tensor_scalar(selr, oh, -1.0, -NEG, ALU.add, ALU.mult))
            link(nc.vector.memset(bsel, NEG))
            for hf in range(2):
                for b in range(4):
                    nc.vector.memset(bsel[32 * b:32 * b + 32, hf, 4 * hf + b:4 * hf + b + 1], 0.0)
            nc.vector.memset(RP1, NEG)
            link(nc.vector.memset(RP2, NEG))
            norm(0, 0, xT, hT)
            dve.wait_ge(s_trow, 16 * 17)
            nc.vector.tensor_copy(RP1[:, NQ:NQ + NTAPS], rowt[:, 0, :])
            link(nc.vector.tensor_copy(RP2[:, NQ:NQ + 4 * (NTAPS - 1) + 1:4], rowt[:, 1, :]))
            for t, rp, n in ((T1, RP1, P + NQ), (T2, RP2, 512 + NQ)):
                link(nc.vector.tensor_scalar(t, rp[:, NQ:NQ + n], oh[:, 0:1], None, ALU.mult))
                for q in range(1, NQ):
                    link(nc.vector.scalar_tensor_tensor(out=t, in0=rp[:, NQ - q:NQ - q + n], scalar=oh[:, q:q + 1], in1=t,
                                                        op0=ALU.mult, op1=ALU.add))
            dve.wait_ge(s_squ, 7)
            dve.wait_ge(s_h, KT)
            nc.vector.tensor_copy(Ts[:, 0:P], T1[:, 0:P])
            nc.vector.tensor_copy(Ts[:, P:P + 512].rearrange("p (r a) -> p r a", r=4),
                                  T2[:, 0:512].rearrange("p (a r) -> p r a", r=4))
            for r in range(NQ):
                nc.vector.tensor_scalar(Ts[:, 640 + r * P:640 + (r + 1) * P], rowt[:, 2, 0:P], selr[:, r:r + 1], None, ALU.add)
            link(nc.vector.tensor_scalar(nw3, selr, rowt[:, 2, NTAPS - 1:NTAPS], None, ALU.add))
            for hf in range(2):
                for g, row in enumerate((T1[:, P:P + NQ], T2[:, 512:512 + NQ], nw3)):
                    last = nc.vector.tensor_tensor(
                        TsN[:, hf, g, :].rearrange("p (b j) -> p b j", b=NB),
                        row.rearrange("p (u j) -> p u j", u=1).to_broadcast([P, NB, NQ]),
                        bsel[:, hf, :].rearrange("p (b u) -> p b u", u=1).to_broadcast([P, NB, NQ]), ALU.add)
            last.then_inc(s_ts, 1)
            unit_emptied(dve, ("qa", 5))
            block_queries(qaT, qblk, 3)
            for name in ("ka", "va"):
                for s in range(3):
                    rows_in((name, s))
            dve.wait_ge(s_ts, 1)
            dve.wait_ge(s_kout[0], 2 * 32)
            dve.wait_ge(s_kout[1], 32)
            attend(("sw", "pw"), 0)
            unit_emptied(dve, ("qb", 3))
            for e in range(2):
                for j in range(4):
                    last = nc.vector.tensor_copy(qbb[HD * e:HD * (e + 1), j, :, NQ * e:NQ * (e + 1)],
                                                 qbT[HD * e:HD * (e + 1), j, SEQ:TOK].rearrange("p (b q) -> p b q", b=NB))
            last.then_inc(s_qk, 1)
            for s in range(2):
                rows_in(("kb", s))
            dve.wait_ge(s_out, 16 * (len(win_cache) + 6))
            for s in range(2):
                rows_in(("vb", s))
            dve.wait_ge(s_kout[0], 3 * 32)
            dve.wait_ge(s_kout[1], 2 * 32)

            def softplus(i):
                s = steps[i]
                n, w = rows(s), span(s)
                lo = lo_of(s) if s[0] == "p" else 0
                bias = sbb[:, s[1]:s[1] + 1] if s[0] == "p" else 0.0
                dve.wait_ge(s_bl, i + 1)
                if i >= 2:
                    dve.wait_ge(s_bc, i - 1)
                sp = spb[0:n, i % 2, lo:lo + w]
                ins = nc.vector.scalar_tensor_tensor(out=sp, in0=bank(i % 3)[0:n, lo:lo + w], scalar=bias,
                                                     in1=zb[0:n, i % 3, lo:lo + w], op0=ALU.add, op1=ALU.max)
                if needs_mask(s):
                    link(ins)
                    m, v = (below[:, :], sp[:, 0:P]) if s[0] == "p" else (newmask[:, s[1], :, :].rearrange("p h q -> p (h q)"), sp)
                    ins = nc.vector.tensor_tensor(v, v, m, ALU.mult)
                ins.then_inc(s_bsp, 1)

            def running(i):
                s = steps[i]
                w = span(s)
                before = earlier(i)
                dve.wait_ge(s_bsp, i + 1)
                if s[0] == "p":
                    lo, k = lo_of(s), place(i)
                    if before is None:
                        prev = max([x for x in range(i) if steps[x][0] == "p"], default=None)
                        if prev is not None:
                            dve.wait_ge(s_bc, prev + 1)
                        link(nc.vector.memset(Rp[:, :, :], 0.0))
                    else:
                        dve.wait_ge(s_bc, before + 1)
                        dve.wait_ge(s_bR, before + 1)
                    nc.vector.tensor_tensor(Rp[:, (k + 1) % 2, lo:512], Rp[:, k % 2, lo:512], spb[:, i % 2, lo:512],
                                            ALU.add).then_inc(s_bR, 1)
                    return
                g = s[2]
                if g < 0:
                    if i >= 1 and s[1] > 0:
                        dve.wait_ge(s_bc, last_of[("s", s[1] - 1)] + 1)
                    link(nc.vector.memset(Rs[:, 0, 4, :], 0.0))
                    nc.vector.tensor_copy(Rs[0:NEWK, 0, 4, :], spb[0:NEWK, i % 2, 0:64]).then_inc(s_bR, 1)
                    return
                dve.wait_ge(s_bc, before + 1)
                dve.wait_ge(s_bR, before + 1)
                for x in range(3, -1, -1):
                    dst = Rs[:, g % 2, x, :] if x else Rs[:, (g + 1) % 2, 4, :]
                    ins = nc.vector.tensor_tensor(dst, Rs[:, g % 2, x + 1, :], spb[:, i % 2, 64 * x:64 * (x + 1)], ALU.add)
                    if x:
                        link(ins)
                ins.then_inc(s_bR, 1)

            def output(i):
                if i not in out_no:
                    return
                s = steps[i]
                dve.wait_ge(s_bv, i + 1)
                if s[0] == "p":
                    _, h, c, _ = s
                    hp = HD * (h % 2)
                    nc.vector.tensor_copy(obT[hp:hp + HD, h // 2, c * 512:(c + 1) * 512],
                                          bank(3 + 2 * c)[hp:hp + HD, :]).then_inc(s_bo, 1)
                    return
                o = bank(4)[:, 0:64].rearrange("p (j n) -> p j n", j=4)
                for e in range(2):
                    last = nc.vector.tensor_copy(obT[HD * e:HD * (e + 1), :, SEQ + NQ * s[1]:SEQ + NQ * (s[1] + 1)],
                                                 o[HD * e:HD * (e + 1), :, NQ * e:NQ * (e + 1)])
                last.then_inc(s_bo, 1)

            for i in range(NS + 3):
                if i < NS:
                    s = steps[i]
                    n, w = rows(s), span(s)
                    lo = lo_of(s) if s[0] == "p" else 0
                    bias = sbb[:, s[1]:s[1] + 1] if s[0] == "p" else 0.0
                    dve.wait_ge(s_bS, i + 1)
                    nc.vector.tensor_scalar(zb[0:n, i % 3, lo:lo + w], bank(i % 3)[0:n, lo:lo + w], bias, BIG, ALU.add,
                                            ALU.min).then_inc(s_bz, 1)
                if 1 <= i <= NS:
                    softplus(i - 1)
                    running(i - 1)
                if i >= 3:
                    output(i - 3)
            for i in range(KT):
                ps = take(("ba", i))
                unit_emptied(dve, ("ga", i))
                nc.vector.tensor_tensor(mgT[:, i, :], ps, sg[:, 0, :], ALU.mult).then_inc(s_ev, 1)
                ps = take(("bb", i))
                unit_emptied(dve, ("gb", i))
                nc.vector.tensor_tensor(sg[:, 1, :], ps, sg[:, 1, :], ALU.mult).then_inc(s_ev, 1)
                unit_emptied(dve, ("bb", i))
                nc.vector.tensor_tensor(mgT[:, i, :], mgT[:, i, :], sg[:, 1, :], ALU.add).then_inc(s_mg, 1)
            dve.wait_ge(s_xe, 2 * TT)
            for i in range(KT):
                nc.vector.tensor_tensor(xT[:, i, :], take(("wo", i)), xT[:, i, :], ALU.add).then_inc(s_ev, 1)
            nc.vector.memset(zeros, 0.0)
            link(nc.vector.memset(qcb, 0.0))
            norm(3, 3, memT, hmT, MEM)
            rows_in(("ck", 0))
            rows_in(("cv", 0))
            norm(1, 1, xT, hT)
            unit_emptied(dve, ("cq", 1))
            block_queries(qcT, qcb, 1)
            attend(("sx", "px"), SEQ // P)
            for i in range(KT):
                nc.vector.tensor_tensor(xT[:, i, :], take(("co", i)), xT[:, i, :], ALU.add).then_inc(s_ev, 1)
            norm(2, 2, xT, hT)
            for c in range(NC + 1):
                if c < NC:
                    for i in range(4):
                        unit_emptied(dve, ("up", c, i))
                        h = hid[:, c % 2, i, :]
                        nc.vector.tensor_tensor(h, h, h, ALU.mult).then_inc(s_hs, 1)
                if c >= 1:
                    if c >= 2:
                        unit_emptied(dve, ("dn", c - 2, KT - 1))
                    for i in range(KT):
                        nc.vector.tensor_tensor(xT[:, i, :], take(("dn", c - 1, i)), xT[:, i, :], ALU.add).then_inc(s_ev, 1)
            norm(4, 4, xT, hT)


_INS = ["x_prompt", "x_sample", "mem_prompt", "cache_win1_k", "cache_win1_v", "cache_win2_k", "cache_win2_v",
        "cache_win3_k", "cache_win3_v", "cache_sb_k", "cache_sb_v", "cache_mem_k", "cache_mem_v", "page_table",
        "norm_mix", "w_in", "w_branch_a", "w_branch_b", "w_out", "rel_bias", "sb_bias", "norm_cross", "norm_mem",
        "w_cq", "w_ck", "w_cv", "w_co", "norm_mlp", "w_up", "w_down", "norm_final"]
_OUTS = [(1, SEQ, D), (NB, NQ, D)]
_OUTS += [(1, 1, min(w, SEQ), HPG, HD) for w, _ in GROUPS for _ in range(2)]
_OUTS += [(1, 1, SEQ, SBH, HD)] * 2 + [(1, 1, MEM, HPG, HD)] * 2
_OUTS += [(1, NB, w, HPG, HD) for w, _ in GROUPS for _ in range(2)]
_OUTS += [(1, NB, NQ, SBH, HD)] * 2


def kernel(**inputs):
    import concourse.bacc as _bacc
    from concourse import mybir as _mybir
    from concourse.bass_utils import run_bass_kernel_spmd as _run

    nc = _bacc.Bacc("TRN2", target_bir_lowering=False, num_devices=1)
    arrays, ins, outs = {}, [], []
    for name in _INS:
        a = np.ascontiguousarray(inputs[name])
        arrays[f"in_{name}"] = a
        ins.append(nc.dram_tensor(f"in_{name}", a.shape, _mybir.dt.from_np(a.dtype), kind="ExternalInput").ap())
    for i, shape in enumerate(_OUTS):
        outs.append(nc.dram_tensor(f"out_{i}", shape, F32, kind="ExternalOutput").ap())
    scratch = (nc.dram_tensor("bias_lines", (12, 1152), F32).ap(), nc.dram_tensor("tap_rows", (12, 3, NTAPS), F32).ap(),
               nc.dram_tensor("line_copies", (12, P, 1152), F32).ap())
    hybrid_decoder_kernel(nc, ins, outs, scratch)
    r = _run(nc, [arrays], core_ids=[0])
    return tuple(r.results[0][f"out_{i}"] for i in range(len(_OUTS)))
```

```python
from contextlib import ExitStack

import numpy as np

import concourse.bass as bass
from concourse import mybir

F32 = mybir.dt.float32
F32R = mybir.dt.float32r
I32 = mybir.dt.int32
ALU = mybir.AluOpType
ACT = mybir.ActivationFunctionType
AX = mybir.AxisListType

P = 128
D = 1024
KT = D // P
SEQ = 1024
NB = 8
NQ = 8
TOK = SEQ + NB * NQ
TT = SEQ // P + 1
HD = 64
GROUPS = ((128, 1), (512, 4), (2048, 16))
HPG = 4
GW = HPG * HD
SBH = 8
SBW = SBH * HD
MEM = 256
PAGES = 16
F = 4096
EPS = 1e-6
NEG = -1e30
BIG = 30.0
LOW = -3.0e38
BUCKETS = 32
MAX_DIST = 2048
NTAPS = 129


def bucket_runs(dil):
    dist = np.arange(NTAPS, dtype=np.int64) * dil
    exact = BUCKETS // 2
    safe = np.maximum(dist, exact).astype(np.float32)
    large = exact + (np.log(safe / exact) / np.log(MAX_DIST / exact) * (BUCKETS - exact)).astype(np.int64)
    b = np.where(dist < exact, dist, np.minimum(large, BUCKETS - 1))
    runs, start = [], 0
    for m in range(1, NTAPS + 1):
        if m == NTAPS or b[m] != b[start]:
            runs.append((start, m, int(b[start])))
            start = m
    return runs


CHUNK = 364
CHUNKS = [(a, min(a + CHUNK, TOK)) for a in range(0, TOK, CHUNK)]


def hybrid_decoder_kernel(nc, ins, outs, scratch):
    (x_prompt, x_sample, mem_prompt, w1k, w1v, w2k, w2v, w3k, w3v, sbk, sbv, memk, memv, page_table,
     norm_mix, w_in, w_ba, w_bb, w_out, rel_bias, sb_bias, norm_cross, norm_mem, w_cq, w_ck, w_cv, w_co,
     norm_mlp, w_up, w_down, norm_final) = ins
    y_p, y_s = outs[0:2]
    p_win = outs[2:8]
    p_sbk, p_sbv, p_memk, p_memv = outs[8:12]
    s_win = outs[12:18]
    s_sbk, s_sbv = outs[18:20]
    win_cache = (w1k, w1v, w2k, w2v, w3k, w3v)
    bias_lines, tap_rows, line_copies = scratch

    REACH = [min(w // P + 1, SEQ // P) for w, _ in GROUPS]
    SEG = [0, REACH[0] * P, (REACH[0] + REACH[1]) * P, sum(REACH) * P]
    LINE = [(n + 1) * P for n in REACH]

    def cols(w, c0, n, k=KT, k0=0):
        return w[0].rearrange("(k p) n -> p k n", p=P)[:, k0:k0 + k, c0:c0 + n]

    slots, slot_of = [], {}

    def slot(key, parts):
        slot_of[key] = len(slots)
        slots.append(parts)

    SLOTW = 2 * P
    offs = {}
    at = 0
    for name, width in (("qa", 768), ("ka", 768), ("va", 768), ("qb", 512), ("kb", 512), ("vb", 512),
                        ("ga", D), ("gb", D)):
        offs[name] = at
        at += width
    for name, n in (("qa", 3), ("ka", 3), ("va", 3), ("qb", 2), ("kb", 2), ("vb", 2)):
        for s in range(n):
            slot((name, s), [(cols(w_in, offs[name] + s * SLOTW, SLOTW), KT, SLOTW)])
    for s in range(4):
        slot(("ga", s), [(cols(w_in, offs["ga"] + s * SLOTW, SLOTW), KT, SLOTW)])
        slot(("gb", s), [(cols(w_in, offs["gb"] + s * SLOTW, SLOTW), KT, SLOTW)])
        slot(("br", s), [(cols(w_ba, s * SLOTW, SLOTW, 2), 2, SLOTW), (cols(w_bb, s * SLOTW, SLOTW, 4), 4, SLOTW)])
    for s in range(4):
        slot(("wo", s), [(cols(w_out, s * SLOTW, SLOTW), KT, SLOTW)])
    slot(("ck", 0), [(cols(w_ck, 0, SLOTW), KT, SLOTW)])
    slot(("cv", 0), [(cols(w_cv, 0, SLOTW), KT, SLOTW)])
    slot(("cq", 0), [(cols(w_cq, 0, SLOTW), KT, SLOTW)])
    slot(("co", 0), [(cols(w_co, 0, D, 2), 2, D)])
    NC = F // SLOTW
    for c in range(NC + 1):
        if c < NC:
            slot(("up", c), [(cols(w_up, c * SLOTW, SLOTW), KT, SLOTW)])
        if c >= 1:
            slot(("dn", c - 1), [(cols(w_down, 0, D, 2, 2 * (c - 1)), 2, D)])
    RING = 3

    units = [(("nm", 0), "v")]
    for name, n, e in (("qa", 6, "a"), ("ka", 6, "a"), ("va", 6, "a"), ("qb", 4, "a"), ("kb", 4, "a"), ("vb", 4, "a")):
        units += [((name, i), e) for i in range(n)]
    for i in range(KT):
        units += [(("ga", i), "a"), (("ba", i), "v"), (("gb", i), "a"), (("bb", i), "v")]
    units += [(("wo", i), "v") for i in range(KT)]
    units += [(("nm", 3), "v"), (("nm", 1), "v")]
    units += [((name, i), "a") for name in ("ck", "cv", "cq") for i in range(2)]
    units += [(("co", i), "v") for i in range(KT)]
    units += [(("nm", 2), "v")]
    for c in range(NC):
        units += [(("up", c, i), "a") for i in range(2)]
        if c >= 1:
            units += [(("dn", c - 1, i), "v") for i in range(KT)]
    units += [(("dn", NC - 1, i), "v") for i in range(KT)]
    units += [(("nm", 4), "v")]
    unit_no = {k: i for i, (k, _) in enumerate(units)}
    count = {"a": 0, "v": 0}
    emptied = []
    for _, e in units:
        count[e] += 1
        emptied.append((e, count[e]))

    NEWK = NB * NQ
    SAMPLE_KEYS = [P, 512, 1024]
    WINW = sum(SAMPLE_KEYS) + 3 * NEWK
    sm = [("sw", h) for h in range(2)]
    sm += [("pw", h, t) for h in range(HPG) for t in range(SEQ // P)]
    sm += [("sx", h) for h in range(2)]
    sm += [("px", h, t) for h in range(HPG) for t in range(SEQ // P)]
    sm_no = {k: i for i, k in enumerate(sm)}

    def blocks(u):
        k = sm[u]
        if k[0] == "pw":
            return [(g, b, P) for g in range(3) for b in range(max(0, k[2] + 1 - REACH[g]), k[2] + 1)]
        if k[0] == "sw":
            return ([(0, 0, P)] + [(1, r, P) for r in range(4)] + [(2, r, P) for r in range(8)]
                    + [(g, -1, NEWK) for g in range(3)])
        return [(0, 0, P), (0, 1, P)]

    def width(u):
        return sum(w for _, _, w in blocks(u))

    def quads(u):
        b = blocks(u)
        return [b[i:i + 4] for i in range(0, len(b), 4)]

    quad_base = [0]
    for u in range(len(sm)):
        quad_base.append(quad_base[-1] + len(quads(u)))

    psteps = [("p", h, c, b) for h in range(SBH) for c in range(2) for b in range(4 * c + 3, -1, -1)]
    ssteps = [("s", b, g) for b in range(NB) for g in range(-1, 4)]
    steps = []
    for x in range(NB):
        steps += [s for s in psteps if s[1] == x] + [s for s in ssteps if s[1] == x]
    NS = len(steps)
    AHEAD = 3
    last_of = {}
    for i, s in enumerate(steps):
        last_of[("p", s[1], s[2]) if s[0] == "p" else ("s", s[1])] = i

    def lo_of(s):
        return max(0, s[3] * P - s[2] * 512)

    def span(s):
        return 512 - lo_of(s) if s[0] == "p" else 256 if s[2] >= 0 else NEWK

    def rows(s):
        return NEWK if s[0] == "s" and s[2] < 0 else P

    def diagonal(s):
        return s[0] == "p" and s[3] >= 4 * s[2]

    with ExitStack() as ctx:
        def sb(name, shape, dt=F32):
            return ctx.enter_context(nc.sbuf_tensor(name, shape, dt))

        def sem(name):
            return ctx.enter_context(nc.semaphore(name))

        psum = ctx.enter_context(nc.psum_tensor("psum", [P, 8 * 512], F32))

        def bank(i, n=1):
            return psum[:, i * 512:(i + n) * 512]

        RX = sb("RX", [P, KT * TOK])
        RR = sb("RR", [P, RING * 2048])

        def pieces(u, n):
            at = 1536 * (u % 2)
            if n <= 512:
                return [(psum[:, at:at + n], lambda t: t[:, 0:n])]
            a = 2 * CHUNK
            return [(psum[:, at:at + 1024].rearrange("p (c n) -> p c n", c=2)[:, :, 0:CHUNK],
                     lambda t: t[:, 0:a].rearrange("p (c n) -> p c n", c=2)),
                    (psum[:, at + 1024:at + 1024 + n - a], lambda t: t[:, a:n])]

        def cut(region, at, *dims):
            n = int(np.prod(dims))
            v = region[:, at:at + n]
            if len(dims) == 2:
                return v.rearrange("p (a b) -> p a b", a=dims[0])
            if len(dims) == 3:
                return v.rearrange("p (a b c) -> p a b c", a=dims[0], b=dims[1])
            if len(dims) == 4:
                return v.rearrange("p (a b c d) -> p a b c d", a=dims[0], b=dims[1], c=dims[2])
            return v

        ident = sb("ident", [P, P])
        ones = sb("ones", [P, P])
        negones = sb("negones", [P, P])
        negtri = sb("negtri", [P, P])
        below = sb("below", [P, P])
        gains = sb("gains", [P, 5, KT])
        sbb = sb("sbb", [P, SBH])
        brow = sb("brow", [1, 4, 64])
        newmask = sb("newmask", [NEWK, NB, SBH, NQ])
        qbb = sb("qbb", [P, 4, NB, 16])
        mx = sb("mx", [P, len(sm), 3])
        nm = sb("nm", [P, len(sm)])
        Zs = sb("Zs", [P, len(sm)])
        rz = sb("rz", [P, len(sm)])
        pg = sb("pg", [1, NB * PAGES], I32)

        early = ExitStack()

        def sb_in(stack, name, shape, dt=F32):
            return stack.enter_context(nc.sbuf_tensor(name, shape, dt))

        RH = sb_in(early, "RH", [P, KT * TOK])
        RQ = sb_in(early, "RQ", [P, 19968])
        RO = sb_in(early, "RO", [P, 6 * TOK])

        xT = cut(RX, 0, KT, TOK)
        hT = cut(RH, 0, KT, TOK)
        ring = cut(RR, 0, RING, 2048)
        oaT = cut(RO, 0, 2, TOK)
        obT = cut(RO, 2 * TOK, 4, TOK)
        qaT = cut(RQ, 0, 6, TOK)
        kaT = cut(RQ, 6 * TOK, 6, TOK)
        va = cut(RQ, 12 * TOK, TT, 768)
        vt = cut(RX, 0, 2, TOK)
        kn = cut(RX, 2 * TOK, 2, TT, GW)
        PTs = cut(RO, 2 * TOK, 4, 512)
        onat = cut(RO, 2 * TOK + 2048, 8, GW)
        qblk = cut(RO, 2 * TOK + 2048, 6, NB, 32)
        KVC = 1280
        OLDK = sum(SAMPLE_KEYS)
        kvw = cut(RX, 0, 3, KVC)
        ktw = cut(RX, 3 * KVC, 2, 512)
        pS = cut(RX, 3 * KVC + 1024, WINW)
        Ts = cut(RX, 6784, OLDK)
        TsN = cut(RO, 2 * TOK + 2048 + 6 * NB * 32, 2, 3, NEWK)
        Th = cut(RX, 0, 1920)
        pP = cut(RX, 1920, 3, 1920)
        AT = KT * TOK + 2 * D
        taps = RQ[0:12, AT:AT + 3 * NTAPS].rearrange("p (g m) -> p g m", g=3)
        relT = RQ[0:12, AT + 387:AT + 387 + BUCKETS]
        LN = AT + 420
        lines = RQ[0:12, LN:LN + sum(LINE)]
        rowt = cut(RQ, LN + 2304, 3, NTAPS)
        RP1 = cut(RQ, LN + 2692, 144)
        RP2 = cut(RQ, LN + 2836, 528)
        ohw = cut(RQ, LN + 3364, 16, 8)
        oh = cut(RQ, LN + 3492, 8)
        selr = cut(RQ, LN + 3500, 8)
        T2 = cut(RQ, LN + 3508, 520)
        T1 = cut(RQ, LN + 4028, 136)
        bsel = cut(RQ, LN + 4164, 2, NB)
        nw3 = cut(RQ, LN + 4180, 8)
        qbT = cut(RQ, 0, 4, TOK)
        kbT = cut(RQ, 4 * TOK, 4, TOK)
        vb = cut(RQ, 8 * TOK, TT, SBW)
        KR, VR = 4, 8
        kpg = cut(RQ, 8 * TOK + TT * SBW, KR, SBW)
        vpg = cut(RQ, 8 * TOK + TT * SBW + KR * SBW, VR, SBW)
        zb = cut(RX, 0, 3, 512)
        spb = cut(RX, 1536, 2, 512)
        Rp = cut(RX, 2560, 2, 512)
        Rs = cut(RX, 3584, 2, 5, 64)
        ab = cut(RX, 4224, 3, 512)
        ktp = cut(RX, 5760, 2, 512)
        mgT = cut(RQ, 0, KT, TOK)
        xn = cut(RQ, KT * TOK, 2, D)
        sg = cut(RQ, KT * TOK + 2 * D, 2, TOK)
        memT = cut(RQ, 0, KT, MEM)
        hmT = cut(RQ, 2048, KT, MEM)
        kmT = cut(RQ, 4096, 2, MEM)
        vmT = cut(RQ, 4608, 2, MEM)
        kvn = cut(RQ, 5120, 2, 2, GW)
        qcT = cut(RQ, 6144, 2, TOK)
        qcb = cut(RQ, 10752, 2, NB, 32)
        zeros = cut(RQ, 11264, MEM)
        pX = cut(RQ, 14080, 3, MEM)
        kvx = cut(RQ, 12032, 2, 512)
        ktx = cut(RQ, 13056, 2, 512)
        sqb = cut(RQ, 15616, 2, TOK)
        rb = cut(RQ, 17792, TOK)

        early.close()
        late = ExitStack()
        hTH = sb_in(late, "hTH", [P, KT, TOK], F32R)
        hTL = sb_in(late, "hTL", [P, KT, TOK], F32R)
        wH = sb_in(late, "wH", [P, 2, 2048], F32R)
        wL = sb_in(late, "wL", [P, 2, 2048], F32R)
        hid = sb_in(late, "hid", [P, TOK])
        with ExitStack() as scratch_stack:
            RN = sb_in(scratch_stack, "RN", [P, 8 * TOK])
        hidH = sb_in(late, "hidH", [P, 2, 2, TOK], F32R)
        hidL = sb_in(late, "hidL", [P, 2, 2, TOK], F32R)
        late.close()
        sqb2 = cut(RN, 0, 2, TOK)
        rb2 = cut(RN, 2 * TOK, TOK)
        hs = cut(RN, 3 * TOK, 3, TOK)
        yst = cut(RN, 5 * TOK, 2, D)

        s_w = [sem(f"weights_landed{i}") for i in range(RING)]
        s_lin = sem("unit_in_psum")
        s_ea = sem("unit_emptied_by_scalar")
        s_ev = sem("unit_emptied_by_vector")
        s_dv = sem("vector_chain")
        s_aa = sem("scalar_chain")
        s_gp = sem("gpsimd_chain")
        s_cst = sem("constants_ready")
        s_small = sem("small_inputs_landed")
        s_x = [sem(f"x_tile_landed{i}") for i in range(2)]
        s_xt = sem("x_tile_turned")
        s_xe = sem("x_tile_in_sbuf")
        s_sq = sem("squares_ready")
        s_squ = sem("squares_used")
        s_var = sem("mean_square_ready")
        s_rt = sem("root_ready")
        s_h = sem("normed_ready")
        s_nt = sem("turned_pair_in_psum")
        s_nv = sem("turned_pair_in_sbuf")
        s_kout = [sem(f"k_rows_stored{i}") for i in range(2)]
        s_out = sem("stores_done")
        s_taps = sem("taps_ready")
        s_lines = sem("lines_stored")
        s_rep = sem("line_copies_stored")
        s_trow = sem("tap_rows_landed")
        s_T = sem("bias_tile_landed")
        s_mv = sem("windows_moved")
        s_ts = sem("sample_bias_ready")
        s_qk = sem("sample_queries_ready")
        s_kv = [sem(f"cache_chunk_landed{i}") for i in range(3)]
        s_ktm = sem("cache_keys_multiplied")
        s_vu = sem("cache_values_used")
        s_kx = [sem(f"memory_chunk_landed{i}") for i in range(2)]
        s_kt = sem("cache_keys_turned")
        s_ktv = sem("cache_keys_in_sbuf")
        s_S = sem("scores_ready")
        s_Sr = sem("scores_read")
        s_nmax = sem("negated_maximum_ready")
        s_p = sem("probabilities_ready")
        s_pn = sem("probabilities_scaled")
        s_pt = sem("probabilities_turned")
        s_pe = [sem("turned_probabilities_in_sbuf_by_vector"), sem("turned_probabilities_in_sbuf_by_scalar")]
        s_o = sem("attention_output_ready")
        s_oe = sem("attention_output_in_sbuf")
        s_ot = sem("attention_output_turned")
        s_ote = sem("attention_output_turned_in_sbuf")
        s_pg = sem("page_numbers_landed")
        s_kp = [sem(f"k_page_landed{i}") for i in range(KR)]
        s_vp = [sem(f"v_page_landed{i}") for i in range(VR)]
        s_bkt = sem("page_keys_turned")
        s_bktv = sem("page_keys_in_sbuf")
        s_bku = sem("page_keys_used")
        s_bS = sem("sb_scores_ready")
        s_bz = sem("sb_scores_clamped")
        s_bl = sem("sb_log_ready")
        s_bsp = sem("sb_softplus_ready")
        s_bR = sem("sb_running_sum_ready")
        s_bc = sem("sb_exponent_ready")
        s_ba = sem("sb_weights_ready")
        s_bam = sem("sb_weights_masked")
        s_bv = sem("sb_values_added")
        s_bo = sem("sb_output_in_sbuf")
        s_mg = sem("branches_merged")
        s_wh = sem("weights_high_ready")
        s_wl = sem("weights_low_ready")
        s_hh = sem("hidden_high_ready")
        s_hl = sem("hidden_low_ready")
        s_nh = sem("normed_high_ready")
        s_hq = sem("hidden_square_ready")
        s_nf = sem("normed_before_its_split")
        s_yt = sem("y_tile_turned")
        s_ye = sem("y_tile_in_sbuf")
        s_yo = [sem(f"y_tile_stored{i}") for i in range(2)]

        def unit_emptied(eng, key):
            e, n = emptied[unit_no[key]]
            eng.wait_ge(s_ea if e == "a" else s_ev, n)

        slot_end = {}
        for name, n in (("qa", 3), ("ka", 3), ("va", 3), ("qb", 2), ("kb", 2), ("vb", 2), ("wo", 4), ("ck", 1), ("cv", 1),
                        ("cq", 1)):
            for s in range(n):
                slot_end[(name, s)] = unit_no[(name, 2 * s + 1)] + 1
        for s in range(4):
            slot_end[("ga", s)] = unit_no[("ga", 2 * s + 1)] + 1
            slot_end[("gb", s)] = unit_no[("gb", 2 * s + 1)] + 1
            slot_end[("br", s)] = unit_no[("bb", 2 * s + 1)] + 1
        slot_end[("co", 0)] = unit_no[("co", KT - 1)] + 1
        slot_keys = sorted(slot_of, key=slot_of.get)
        split_no = {}
        for c in range(NC + 1):
            if c < NC:
                split_no[("up", c)] = len(split_no)
            if c >= 1:
                split_no[("dn", c - 1)] = len(split_no)
        split_keys = list(split_no)
        w_count, total = [], [0] * RING
        for i, parts in enumerate(slots):
            total[i % RING] += 16 * len(parts)
            w_count.append(total[i % RING])

        turned = [(n, s) for n, c in (("ka", 3), ("va", 3), ("kb", 2), ("vb", 2)) for s in range(c)]
        turn_base = {k: 5 * i for i, k in enumerate(turned)}
        turn_base[("ck", 0)] = 5 * len(turned)
        turn_base[("cv", 0)] = 5 * len(turned) + 1
        k_slots = [k for k in turned if k[0][0] == "k"]

        wchunks = [("sw", hf, kv, b, part) for hf in range(2) for kv in range(2) for b in range(4) for part in range(3)]
        chunks = wchunks + [("sx", hf, kv, b, 0) for hf in range(2) for kv in range(2) for b in range(4)]
        chunk_no = {c: i for i, c in enumerate(chunks)}
        NWC = len(wchunks)

        def chunk_buf(n):
            return kvw[:, n % 3, :] if n < NWC else kvx[:, n % 2, :]

        def kv_wait(eng, n):
            if n < NWC:
                eng.wait_ge(s_kv[n % 3], 32 * (n // 3 + 1))
            else:
                eng.wait_ge(s_kx[n % 2], 16 * ((n - NWC) // 2 + 1))

        def chunk_tiles(c):
            if c[0] == "sx":
                return [(0, 0), (1, 1)]
            if c[4] == 0:
                return [(r, r) for r in range(5)]
            return [(r, 5 + 4 * (c[4] - 1) + r) for r in range(4)]

        turns, chunk_freed = [], {}
        values = 0
        for n, c in enumerate(chunks):
            if c[2] == 0:
                t = chunk_tiles(c)
                turns += [(n, t[i:i + 2]) for i in range(0, len(t), 2)]
                chunk_freed[n] = ("k", len(turns))
            else:
                values += 1
                chunk_freed[n] = ("v", values)

        def chunk_free(eng, n):
            kind, v = chunk_freed[n]
            eng.wait_ge(s_kt if kind == "k" else s_vu, v)

        outs_b = [i for i in range(NS) if i in last_of.values()]
        out_no = {i: n for n, i in enumerate(outs_b)}

        norm_order = [0, 3, 1, 2, 4]
        V_ROW_STORES = 2 * 5

        def p_of(u):
            kind = sm[u][0]
            return pS if kind == "sw" else pP[:, u % 3, :] if kind == "pw" else pX[:, u % 3, :]

        def sb_bank(i):
            return bank((0, 1, 2, 5)[i % 4])

        samples = [u for u, k in enumerate(sm) if k[0][0] == "s"]
        sample_no = {u: i for i, u in enumerate(samples)}

        def quad_evacuate(eng, copy, u, j):
            q = quad_base[u] + j
            if (q % 2 == 0) != (copy == nc.vector.tensor_copy):
                return
            eng.wait_ge(s_pt, q + 1)
            if u >= 1:
                eng.wait_ge(s_o, u)
            n = quads(u)[j][0][2]
            runs = [(x, w) for x, (_, _, w) in enumerate(quads(u)[j])]
            wide = [x for x, w in runs if w == P]
            thin = [x for x, w in runs if w < P]
            for xs, n in ((wide, P), (thin, NEWK)):
                if xs:
                    a, b = xs[0] * P, (xs[-1] + 1) * P
                    at = 512 * (4 + q % 2)
                    last = copy(PTs[0:n, j, a:b], psum[0:n, at + a:at + b])
            last.then_inc(s_pe[q % 2], 1)

        def needs_mask(s):
            return diagonal(s) or (s[0] == "s" and s[2] < 0)

        mask_no, n = {}, 0
        for i, s in enumerate(steps):
            if needs_mask(s):
                mask_no[i] = n
                n += 1

        def chain_of(s):
            return ("p", s[1], s[2]) if s[0] == "p" else ("s", s[1])

        before_of, place_of, seen = [], [], {}
        for i, s in enumerate(steps):
            c = chain_of(s)
            before_of.append(seen[c][0] if c in seen else None)
            place_of.append(seen[c][1] + 1 if c in seen else 0)
            seen[c] = (i, place_of[-1])

        def earlier(i):
            return before_of[i]

        def place(i):
            return place_of[i]

        def out_before(i):
            s = steps[i]
            if s[0] == "s":
                return out_no[last_of[("s", s[1] - 1)]] if s[1] else None
            if s[2]:
                return out_no[last_of[("p", s[1], 0)]]
            return out_no[last_of[("p", s[1] - 1, 1)]] if s[1] else None

        block = ctx.enter_context(nc.Block())

        @block.sync
        def _(sp):
            def weights(key):
                i = slot_of[key]
                if i >= RING:
                    before = slot_keys[i - RING]
                    if before in split_no:
                        sp.wait_ge(s_wl, split_no[before] + 1)
                    else:
                        sp.wait_ge(s_lin, slot_end[before])
                at = 0
                for src, k, n in slots[i]:
                    dst = ring[:, i % RING, at:at + k * n].rearrange("p (k n) -> p k n", k=k)
                    sp.dma_start(dst, src).then_inc(s_w[i % RING], 16)
                    at += k * n

            def x_tile(i):
                if i >= 2:
                    sp.wait_ge(s_xt, i - 1)
                t = i % TT
                if i < 2 * TT:
                    src = x_prompt[0, t * P:(t + 1) * P, :] if t < TT - 1 else x_sample.rearrange("b q d -> (b q) d")
                else:
                    t = i - 2 * TT
                    src = mem_prompt[0, t * P:(t + 1) * P, :]
                sp.dma_start(xn[0:src.shape[0], i % 2, :], src).then_inc(s_x[i % 2], 16)

            sp.dma_start(pg[:, :], page_table.rearrange("(o b) p -> o (b p)", o=1)).then_inc(s_pg, 16)
            for t in range(TT):
                x_tile(t)
                if t < RING:
                    weights(("qa", t))
            for name in ("ka", "va"):
                for s in range(3):
                    weights((name, s))
            sp.wait_ge(s_nv, turn_base[("va", 2)] + 5)
            sp.wait_ge(s_kout[0], 2 * 32)
            sp.wait_ge(s_kout[1], 32)
            for n, (_, hf, kv, b, part) in enumerate(wchunks):
                if n >= 3:
                    chunk_free(sp, n - 3)
                q = 4 * hf + b
                if part == 0:
                    sp.dma_start(kvw[:, n % 3, 0:GW],
                                 win_cache[kv][0, q].rearrange("k h d -> k (h d)")).then_inc(s_kv[n % 3], 16)
                    sp.dma_start(kvw[:, n % 3, GW:5 * GW],
                                 win_cache[2 + kv][0, q].rearrange("(p r) h d -> p (r h d)", r=4)).then_inc(s_kv[n % 3], 16)
                else:
                    r0 = 4 * (part - 1)
                    src = win_cache[4 + kv][0, q].rearrange("(p r) h d -> p r (h d)", r=16)[:, r0:r0 + 4, :]
                    sp.dma_start(kvw[:, n % 3, 0:4 * GW].rearrange("p (r f) -> p r f", r=4), src).then_inc(s_kv[n % 3], 32)
            sp.wait_ge(s_rep, 16 * 3 * HPG)
            sp.wait_ge(s_oe, 2)
            for h in range(HPG):
                if h >= 1:
                    sp.wait_ge(s_Sr, sm_no[("pw", h - 1, 7)] + 1)
                for g in range(3):
                    copy = line_copies[g * HPG + h]
                    src = bass.AP(tensor=copy.tensor, offset=copy.offset + P - 1,
                                  ap=[[max(LINE) - 1, P], [1, REACH[g] * P]])
                    sp.dma_start(Th[:, SEG[g]:SEG[g + 1]], src).then_inc(s_T, 16)
            for name in ("qb", "kb", "vb"):
                for s in range(2):
                    weights((name, s))
            def gate_weights(s):
                for name in ("ga", "gb", "br"):
                    weights((name, s))

            gate_weights(0)
            sp.wait_ge(s_pg, 16)
            sp.wait_ge(s_ote, SEQ // P)
            sp.wait_ge(s_out, 16 * 6)
            def page_of(n):
                i = (n // PAGES) * PAGES + PAGES - 1 - n % PAGES
                return sp.value_load(pg[0:1, i:i + 1], min_val=0, max_val=sbk.shape[1] - 1)

            def step_of(n):
                return steps.index(("s", n // PAGES, (n % PAGES) // 4))

            loads = [((step_of(n - KR) - AHEAD if n >= KR else -AHEAD, 0, n), "k", n) for n in range(NB * PAGES)]
            loads += [((step_of(n - VR) + 1 if n >= VR else -AHEAD, 1, n), "v", n) for n in range(NB * PAGES)]
            for _, kind, n in sorted(loads):
                page = page_of(n)
                if kind == "k":
                    if n >= KR:
                        sp.wait_ge(s_bkt, n - KR + 1)
                    sp.dma_start(kpg[:, n % KR, :],
                                 sbk[0, bass.ds(page, 1)].rearrange("o t h d -> (o t) (h d)")).then_inc(s_kp[n % KR], 16)
                else:
                    if n >= VR:
                        sp.wait_ge(s_bv, step_of(n - VR) + 1)
                    sp.dma_start(vpg[:, n % VR, :],
                                 sbv[0, bass.ds(page, 1)].rearrange("o t h d -> (o t) (h d)")).then_inc(s_vp[n % VR], 16)
            sp.wait_ge(s_bv, NS)
            sp.wait_ge(s_out, 16 * V_ROW_STORES)
            for s in range(4):
                if s:
                    gate_weights(s)
                x_tile(TT + 2 * s)
                x_tile(TT + 2 * s + 1)
            x_tile(2 * TT - 1)
            for s in range(4):
                weights(("wo", s))
            for t in range(2):
                x_tile(2 * TT + t)
            for name in ("ck", "cv", "cq"):
                weights((name, 0))
            unit_emptied(sp, ("wo", KT - 1))
            for n in range(NWC, len(chunks)):
                _, hf, kv, b, _ = chunks[n]
                if n >= NWC + 2:
                    chunk_free(sp, n - 2)
                sp.dma_start(chunk_buf(n),
                             (memk, memv)[kv][0, 4 * hf + b].rearrange("(p r) h d -> p (r h d)", r=2)).then_inc(s_kx[n % 2], 16)
            weights(("co", 0))
            for key in slot_keys:
                if key[0] in ("up", "dn"):
                    weights(key)

        @block.gpsimd
        def _(gp):
            chain = [0]

            def link(ins):
                chain[0] += 1
                ins.then_inc(s_gp, 1)
                gp.wait_ge(s_gp, chain[0])

            stored = [0]

            def store(dst, src):
                gp.dma_start(dst, src).then_inc(s_out, 16)
                stored[0] += 1

            with nc.allow_non_contiguous_dma(reason="small transposed inputs"):
                gp.dma_start(relT, rel_bias.rearrange("b h -> h b")).then_inc(s_small, 16)
                for i, g in enumerate((norm_mix, norm_cross, norm_mlp, norm_mem)):
                    gp.dma_start(gains[:, i, :], g[0].rearrange("(k p) -> p k", p=P)).then_inc(s_small, 16)
                gp.dma_start(gains[:, 4, :], norm_final.rearrange("(k p) -> p k", p=P)).then_inc(s_small, 16)
                gp.dma_start(sbb[:, :], sb_bias[0:1, :].to_broadcast([P, SBH])).then_inc(s_small, 16)
            link(nc.gpsimd.memset(ones[:, :], 1.0))
            link(nc.gpsimd.memset(negones[:, :], -1.0))
            link(nc.gpsimd.memset(ident[:, :], 0.0))
            link(nc.gpsimd.affine_select(out=ident[:, :], in_=ident[:, :], compare_op=ALU.not_equal, fill=1.0, base=0,
                                         pattern=[[-1, P]], channel_multiplier=1))
            link(nc.gpsimd.affine_select(out=negtri[:, :], in_=negones[:, :], compare_op=ALU.is_ge, fill=0.0, base=0,
                                         pattern=[[-1, P]], channel_multiplier=1))
            link(nc.gpsimd.affine_select(out=below[:, :], in_=ones[:, :], compare_op=ALU.is_gt, fill=0.0, base=0,
                                         pattern=[[1, P]], channel_multiplier=-1))

            def keep_new(t, b0, nb):
                link(nc.gpsimd.affine_select(out=t, in_=t, compare_op=ALU.is_ge, fill=0.0, base=-NQ * b0,
                                             pattern=[[-NQ, nb], [0, SBH], [0, NQ]], channel_multiplier=1))
                return nc.gpsimd.affine_select(out=t, in_=t, compare_op=ALU.is_gt, fill=0.0, base=NQ * b0,
                                               pattern=[[NQ, nb], [0, SBH], [1, NQ]], channel_multiplier=-1)

            link(nc.gpsimd.memset(newmask[:, :, :, :], 1.0))
            link(keep_new(newmask[:, :, :, :], 0, NB))
            link(nc.gpsimd.memset(ohw, 0.0))
            link(nc.gpsimd.affine_select(out=ohw, in_=ohw, compare_op=ALU.not_equal, fill=1.0, base=0,
                                         pattern=[[-8, 16], [-1, 8]], channel_multiplier=1))
            link(nc.gpsimd.memset(qblk, 0.0))
            nc.gpsimd.memset(qbb[:, :, :, :], 0.0).then_inc(s_cst, 1)

            gp.wait_ge(s_taps, 1)
            for g in range(3):
                at = LN + sum(LINE[:g])
                gp.dma_start(bias_lines[g * HPG:(g + 1) * HPG, 0:LINE[g]],
                             RQ[g * HPG:(g + 1) * HPG, at:at + LINE[g]]).then_inc(s_lines, 16)
            gp.wait_ge(s_lines, 16 * 3)
            for g in range(3):
                for h in range(HPG):
                    r = g * HPG + h
                    gp.dma_start(line_copies[r, :, 0:LINE[g]],
                                 bias_lines[r:r + 1, 0:LINE[g]].to_broadcast([P, LINE[g]])).then_inc(s_rep, 16)
            gp.dma_start(tap_rows.rearrange("h g m -> h (g m)"), taps.rearrange("p g m -> p (g m)")).then_inc(s_trow, 16)
            gp.wait_ge(s_trow, 16)
            for i in range(4):
                for h in range(HPG):
                    a = tap_rows[h:h + 1, 0:1, :]
                    src = bass.AP(tensor=a.tensor, offset=a.offset, ap=[[0, NQ], [(HPG * 3 + 1) * NTAPS, 3], [1, NTAPS]])
                    p0 = 32 * i + NQ * h
                    gp.dma_start(rowt[p0:p0 + NQ, :, :], src).then_inc(s_trow, 16)

            def rows_out(key, src, put):
                name, s = key
                if name in ("ka", "va"):
                    kv = 0 if name == "ka" else 1
                    dst, w = p_win[2 * s + kv], s_win[2 * s + kv]
                    t0 = TT - 1 - dst.shape[2] // P
                    put(dst[0, 0].rearrange("(t p) h d -> p t (h d)", p=P), src[:, t0:TT - 1, :])
                    n = w.shape[2]
                    put(w[0, :, n - NQ:n].rearrange("b j h d -> b j (h d)"), src[0:NEWK, TT - 1, :])
                else:
                    dst, w = (p_sbk, s_sbk) if name == "kb" else (p_sbv, s_sbv)
                    h0 = s * 4
                    put(dst[0, 0, :, h0:h0 + 4].rearrange("(t p) h d -> p t (h d)", p=P), src[:, 0:TT - 1, :])
                    put(w[0, :, :, h0:h0 + 4].rearrange("b j h d -> (b j) (h d)"), src[0:NEWK, TT - 1, :])

            for key in turned:
                gp.wait_ge(s_nv, turn_base[key] + 5)
                if key[0][0] == "k":
                    i = k_slots.index(key)
                    rows_out(key, kn[:, i % 2, :, :], lambda d, s: gp.dma_start(d, s).then_inc(s_kout[i % 2], 16))
                else:
                    src = va if key[0] == "va" else vb
                    rows_out(key, src[:, :, key[1] * GW:(key[1] + 1) * GW], store)
            for i, s in enumerate(steps):
                if not needs_mask(s):
                    continue
                gp.wait_ge(s_ba, i + 1)
                if s[0] == "p":
                    t = ab[:, i % 3, lo_of(s):lo_of(s) + P]
                    nc.gpsimd.affine_select(out=t, in_=t, compare_op=ALU.is_gt, fill=0.0, base=0, pattern=[[1, P]],
                                            channel_multiplier=-1).then_inc(s_bam, 1)
                else:
                    t = ab[0:NEWK, i % 3, 0:64].rearrange("p (b h q) -> p b h q", b=1, h=SBH)
                    keep_new(t, s[1], 1).then_inc(s_bam, 1)
            for i, dst in enumerate((p_memk, p_memv)):
                gp.wait_ge(s_nv, 5 * len(turned) + i + 1)
                store(dst[0, 0].rearrange("(t p) h d -> p t (h d)", p=P), kvn[:, i, :, :])
            for t in range(TT):
                gp.wait_ge(s_ye, t + 1)
                n = P if t < TT - 1 else NEWK
                dst = y_p[0, t * P:(t + 1) * P, :] if t < TT - 1 else y_s.rearrange("b q d -> (b q) d")
                gp.dma_start(dst, yst[0:n, t % 2, :]).then_inc(s_yo[t % 2], 16)
            gp.wait_ge(s_yo[0], 16 * 5)
            gp.wait_ge(s_yo[1], 16 * 4)
            gp.wait_ge(s_out, 16 * stored[0])
            gp.wait_ge(s_mv, 16 * NB * len(win_cache))
            gp.wait_ge(s_kout[0], 3 * 32)
            gp.wait_ge(s_kout[1], 2 * 32)

        @block.tensor
        def _(pe):
            def banks(u, n):
                at = 1536 * (u % 2)
                ends = CHUNKS if n == TOK else [(0, n)]
                return [(psum[:, at + 512 * c:at + 512 * c + b - a], a, b) for c, (a, b) in enumerate(ends)]

            def free_set(u):
                if u >= 2:
                    e, n = emptied[u - 2]
                    pe.wait_ge(s_ea if e == "a" else s_ev, n)

            def unit(key, lhs, rhs, n=TOK, normed=None):
                u = unit_no[key]
                free_set(u)
                for k, w in enumerate(lhs):
                    if normed is not None:
                        pe.wait_ge(s_h, KT * normed + k + 1)
                    for out, a, b in banks(u, n):
                        last = pe.matmul(out, w, rhs[:, k, a:b], start=(k == 0), stop=(k == len(lhs) - 1))
                last.then_inc(s_lin, 1)

            def unit_split(key, high, low, rhs_high, rhs_low, normed=None):
                u = unit_no[key]
                free_set(u)
                for k, (wh, wl) in enumerate(zip(high, low)):
                    if normed is not None:
                        pe.wait_ge(s_h, KT * normed + k + 1)
                    for out, a, b in banks(u, TOK):
                        pe.matmul(out, wh, rhs_high[:, k, a:b], start=(k == 0), stop=False)
                    for out, a, b in banks(u, TOK):
                        pe.matmul(out, wh, rhs_low[:, k, a:b], start=False, stop=False)
                    for out, a, b in banks(u, TOK):
                        last = pe.matmul(out, wl, rhs_high[:, k, a:b], start=False, stop=(k == len(high) - 1))
                last.then_inc(s_lin, 1)

            def use_slot(key):
                i = slot_of[key]
                pe.wait_ge(s_w[i % RING], w_count[i])
                return ring[:, i % RING, :]

            def split_slot(key):
                n = split_no[key]
                pe.wait_ge(s_wl, n + 1)
                return wH[:, n % 2, :], wL[:, n % 2, :]

            def column_tile(view, k, n, c, at=0):
                w = view[:, at:at + k * n].rearrange("p (k n) -> p k n", k=k)
                return [w[:, j, c * P:(c + 1) * P] for j in range(k)]

            def norm(i, n=TOK):
                u = unit_no[("nm", i)]
                free_set(u)
                r = norm_order.index(i)
                sq = sqb2 if i in (2, 4) else sqb
                for k in range(KT):
                    pe.wait_ge(s_sq, KT * r + k + 1)
                    for out, a, b in banks(u, n):
                        last = pe.matmul(out, ones[:, :], sq[:, k % 2, a:b], start=(k == 0), stop=(k == KT - 1))
                    last.then_inc(s_squ if k < KT - 1 else s_lin, 1)

            def x_turn(i):
                pe.wait_ge(s_x[i % 2], 16 * (i // 2 + 1))
                if i >= 1:
                    pe.wait_ge(s_xe, i)
                n = NEWK if i in (TT - 1, 2 * TT - 1) else P
                for k in range(KT):
                    at = 3072 + k * P
                    last = pe.transpose(psum[:, at:at + n], xn[0:n, i % 2, k * P:(k + 1) * P], ident[0:n, 0:n])
                last.then_inc(s_xt, 1)

            def turn_rows(key):
                name, s = key
                for c in range(2):
                    unit_emptied(pe, (name, 2 * s + c))
                for j in range(5 if name[0] != "c" else 1):
                    i = turn_base[key] + j
                    if i >= 2:
                        pe.wait_ge(s_nv, i - 1)
                    for t in range(2 * j, min(2 * j + 2, TT)):
                        n = P if t < TT - 1 else NEWK
                        for c in range(2):
                            src = {"ka": kaT, "kb": kbT, "ck": kmT}.get(name)
                            src = src[:, 2 * s + c, :] if src is not None else (vmT if name == "cv" else vt)[:, c, :]
                            o = 512 * (6 + i % 2) + (t - 2 * j) * GW + c * P
                            last = pe.transpose(psum[0:n, o:o + P], src[:, t * P:t * P + n], ident[:, :])
                    last.then_inc(s_nt, 1)

            def project(names):
                before = None
                for name, n in names:
                    for s in range(n):
                        v = use_slot((name, s))
                        for c in range(2):
                            unit((name, 2 * s + c), column_tile(v, KT, SLOTW, c), hT,
                                 normed=0 if (name, s, c) == ("qa", 0, 0) else None)
                        if before:
                            turn_rows(before)
                        before = (name, s) if name[0] != "q" else None
                turn_rows(before)

            def prompt_scores(u):
                kind, h, t = sm[u]
                if u >= 1:
                    pe.wait_ge(s_Sr, u)
                hp = HD * (h % 2)
                runs, col = [], 0
                for g, b, w in blocks(u):
                    if runs and runs[-1][0] == g and col % 512:
                        runs[-1][3] += w
                    else:
                        runs.append([g, b, col, w])
                    col += w
                for g, b, col, w in runs:
                    q, k = (qaT, kaT) if kind == "pw" else (qcT, kmT)
                    j = 2 * g + h // 2
                    last = pe.matmul(psum[:, col:col + w], q[hp:hp + HD, j, t * P:(t + 1) * P],
                                     k[hp:hp + HD, j, b * P:b * P + w], start=True, stop=True)
                last.then_inc(s_S, 1)

            def sample_scores(u):
                kind, hf = sm[u]
                if u >= 1:
                    pe.wait_ge(s_Sr, u)
                    pe.wait_ge(s_oe, u)
                mine = [i for i, (n, _) in enumerate(turns) if chunks[n][0:2] == (kind, hf)]
                qs = qblk if kind == "sw" else qcb
                kts = ktw if kind == "sw" else ktx

                def multiply(i):
                    n, tiles = turns[i]
                    b = chunks[n][3]
                    pe.wait_ge(s_ktv, i + 1)
                    for x, (_, blk) in enumerate(tiles):
                        g = blocks(u)[blk][0]
                        for pair in range(2):
                            last = pe.matmul(psum[32 * b:32 * b + 32, blk * P:(blk + 1) * P],
                                             qs[:, 2 * g + pair, 4 * hf + b, :],
                                             kts[:, i % 2, (2 * x + pair) * P:(2 * x + pair + 1) * P],
                                             start=(pair == 0), stop=(pair == 1))
                    if kind == "sw" and i + 1 < len(turns) and turns[i + 1][0] != n and chunks[n][4] == 2:
                        for g in range(3):
                            for pair in range(2):
                                at = OLDK + g * NEWK
                                last = pe.matmul(psum[32 * b:32 * b + 32, at:at + NEWK], qs[:, 2 * g + pair, 4 * hf + b, :],
                                                 kaT[:, 2 * g + pair, SEQ:TOK], start=(pair == 0), stop=(pair == 1))
                    last.then_inc(s_ktm, 1)

                for i in mine:
                    n, tiles = turns[i]
                    kv_wait(pe, n)
                    if i >= 2:
                        pe.wait_ge(s_ktv, i - 1)
                    for x, (r, _) in enumerate(tiles):
                        for pair in range(2):
                            at = 512 * (6 + i % 2) + (2 * x + pair) * P
                            last = pe.transpose(psum[:, at:at + P],
                                                chunk_buf(n)[:, r * GW + pair * P:r * GW + (pair + 1) * P], ident[:, :])
                    last.then_inc(s_kt, 1)
                    if i > mine[0]:
                        multiply(i - 1)
                multiply(mine[-1])
                pe.drain().then_inc(s_S, 1)

            def turn_quad(u, j):
                q = quad_base[u] + j
                if q >= 2:
                    pe.wait_ge(s_pe[q % 2], q // 2)
                for x, (_, _, w) in enumerate(quads(u)[j]):
                    col = sum(b[2] for b in blocks(u)[0:4 * j + x])
                    at = 512 * (4 + q % 2) + x * P
                    last = pe.transpose(psum[0:w, at:at + P], p_of(u)[:, col:col + w], ident[:, :])
                last.then_inc(s_pt, 1)

            def prompt_values(u, following=None):
                kind, h, t = sm[u]
                pe.wait_ge(s_p, u + 1)
                n = len(quads(u))
                o = psum[:, 512 * (6 + u % 2):512 * (6 + u % 2) + HD]

                def multiply(j):
                    q = quad_base[u] + j
                    pe.wait_ge(s_pe[q % 2], q // 2 + 1)
                    if j == 0 and u >= 2:
                        pe.wait_ge(s_oe, u - 1)
                    for x, (g, b, _) in enumerate(quads(u)[j]):
                        v = va[:, b, g * GW + h * HD:g * GW + (h + 1) * HD] if kind == "pw" else kvn[:, 1, b, h * HD:(h + 1) * HD]
                        last = pe.matmul(o, PTs[:, j, x * P:(x + 1) * P], v, start=(4 * j + x == 0),
                                         stop=(4 * j + x == len(blocks(u)) - 1))
                    return last

                for j in range(min(2, n)):
                    turn_quad(u, j)
                if following is not None:
                    prompt_scores(following)
                for j in range(n):
                    last = multiply(j)
                    if j + 2 < n:
                        turn_quad(u, j + 2)
                last.then_inc(s_o, 1)

            def sample_values(u):
                kind, hf = sm[u]
                pe.wait_ge(s_pn, sample_no[u] + 1)
                for j in range(len(quads(u))):
                    turn_quad(u, j)
                for j in range(max(0, len(quads(u)) - 2), len(quads(u))):
                    q = quad_base[u] + j
                    pe.wait_ge(s_pe[q % 2], q // 2 + 1)
                if u >= 2:
                    pe.wait_ge(s_oe, u - 1)
                pe.wait_ge(s_ktv, max(i for i, (n, _) in enumerate(turns) if chunks[n][0:2] == (kind, hf)) + 1)
                first = True
                for b in range(4):
                    for part in range(3 if kind == "sw" else 1):
                        n = chunk_no[(kind, hf, 1, b, part)]
                        kv_wait(pe, n)
                        tiles = [(chunk_buf(n)[:, r * GW:(r + 1) * GW], blk) for r, blk in chunk_tiles(chunks[n])]
                        if kind == "sw" and part == 2:
                            tiles = [(va[0:NEWK, TT - 1, g * GW:(g + 1) * GW], 13 + g) for g in range(3)] + tiles
                        for v, blk in tiles:
                            w = blocks(u)[blk][2]
                            for pair in range(2):
                                at = 512 * (6 + u % 2) + (2 * b + pair) * 16
                                pt = PTs[0:w, blk // 4, (blk % 4) * P + 32 * b + 16 * pair:(blk % 4) * P + 32 * b + 16 * pair + 16]
                                last = pe.matmul(psum[:, at:at + 16], v[:, pair * P:(pair + 1) * P], pt, start=first,
                                                 stop=(blk == tiles[-1][1] and part == (2 if kind == "sw" else 0)),
                                                 skip_group_check=True)
                                first = False
                        last.then_inc(s_vu, 1)
                pe.drain().then_inc(s_o, 1)

            def attend(kinds):
                mine = [u for u, k in enumerate(sm) if k[0] in kinds]
                for u in mine:
                    if sm[u][0][0] == "s":
                        sample_scores(u)
                        sample_values(u)
                        continue
                    if sm[u - 2][0] != sm[u][0]:
                        prompt_scores(u)
                    else:
                        prompt_values(u - 2, u)
                prompt_values(mine[-2])
                prompt_values(mine[-1])

            def turn_outputs(first_oe, n0):
                pe.wait_ge(s_oe, first_oe)
                for e in range(2):
                    m = (quad_base[first_oe] - 1 - e)
                    pe.wait_ge(s_pe[m % 2], m // 2 + 1)
                for t in range(SEQ // P):
                    if t >= 2:
                        pe.wait_ge(s_ote, n0 + t - 1)
                    for c in range(2):
                        at = 512 * (4 + t % 2) + c * P
                        last = pe.transpose(psum[:, at:at + P], onat[:, t, c * P:(c + 1) * P], ident[:, :])
                    last.then_inc(s_ot, 1)

            def sb_scores(i):
                s = steps[i]
                if i >= 4:
                    pe.wait_ge(s_ba, i - 3)
                out = sb_bank(i)
                if s[0] == "p":
                    _, h, c, b = s
                    hp, lo = HD * (h % 2), lo_of(s)
                    pe.matmul(out[:, lo:512], kbT[hp:hp + HD, h // 2, b * P:(b + 1) * P],
                              qbT[hp:hp + HD, h // 2, c * 512 + lo:(c + 1) * 512], start=True, stop=True).then_inc(s_bS, 1)
                    return
                _, b, g = s
                n = rows(s)
                w = span(s)
                pe.matmul(out[0:n, 0:w], ones[0:1, 0:n], brow[0:1, :, :].rearrange("o j n -> o (j n)")[:, 0:w],
                          start=True, stop=False, skip_group_check=True)
                if g < 0:
                    for pair in range(4):
                        last = pe.matmul(out[0:n, pair * 16:(pair + 1) * 16], kbT[:, pair, SEQ:TOK], qbb[:, pair, b, :],
                                         start=False, stop=(pair == 3), skip_group_check=True)
                    last.then_inc(s_bS, 1)
                    return

                def page_scores(x):
                    n = b * PAGES + 4 * g + x
                    pe.wait_ge(s_bktv, n + 1)
                    for pair in range(4):
                        at = (3 - x) * 64 + pair * 16
                        last = pe.matmul(out[:, at:at + 16], ktp[:, n % 2, pair * P:(pair + 1) * P], qbb[:, pair, b, :],
                                         start=False, stop=(x == 3), skip_group_check=True)
                    last.then_inc(s_bku if x < 3 else s_bS, 1)

                for x in range(4):
                    n = b * PAGES + 4 * g + x
                    pe.wait_ge(s_kp[n % KR], 16 * (n // KR + 1))
                    if n >= 2:
                        pe.wait_ge(s_bktv, n - 1)
                    for pair in range(4):
                        at = 512 * (6 + n % 2) + pair * P
                        last = pe.transpose(psum[:, at:at + P], kpg[:, n % KR, pair * P:(pair + 1) * P], ident[:, :])
                    last.then_inc(s_bkt, 1)
                    if x >= 1:
                        page_scores(x - 1)
                page_scores(3)

            def sb_exponent(i):
                s = steps[i]
                n = rows(s)
                lo = lo_of(s) if s[0] == "p" else 0
                hi = lo + span(s)
                out = sb_bank(i)[0:n, lo:hi]
                before = earlier(i)
                pe.wait_ge(s_bsp, i + 1)
                last = pe.matmul(out, negtri[0:n, 0:n], spb[0:n, i % 2, lo:hi], start=False, stop=before is None,
                                 skip_group_check=True)
                if before is not None:
                    if s[0] == "p":
                        pe.wait_ge(s_bR, before + 1)
                        r = Rp[:, place(i) % 2, lo:hi]
                    else:
                        pe.wait_ge(s_bR, i + 1)
                        r = Rs[:, s[2] % 2, 1:5, :].rearrange("p j n -> p (j n)")
                    last = pe.matmul(out, negones[:, :], r, start=False, stop=True, skip_group_check=True)
                last.then_inc(s_bc, 1)

            def sb_values(i):
                s = steps[i]
                pe.wait_ge(s_ba, i + 1)
                if needs_mask(s):
                    pe.wait_ge(s_bam, mask_no[i] + 1)
                first = earlier(i) is None
                if s[0] == "p":
                    _, h, c, b = s
                    hp, lo = HD * (h % 2), lo_of(s)
                    if first and out_before(i) is not None:
                        pe.wait_ge(s_bo, out_before(i) + 1)
                    o = bank(3)[hp:hp + HD, lo:512]
                    pe.matmul(o, vb[:, b, h * HD:(h + 1) * HD], ab[:, i % 3, lo:512], start=first, stop=(b == 0),
                              skip_group_check=True).then_inc(s_bv, 1)
                    return
                _, b, g = s
                if first and out_before(i) is not None:
                    pe.wait_ge(s_bo, out_before(i) + 1)
                for x in range(4 if g >= 0 else 1):
                    n = b * PAGES + 4 * g + x
                    if g >= 0:
                        pe.wait_ge(s_vp[n % VR], 16 * (n // VR + 1))
                    for pair in range(4):
                        at = 16 * pair
                        if g < 0:
                            v, a = vb[0:NEWK, TT - 1, pair * P:(pair + 1) * P], ab[0:NEWK, i % 3, at:at + 16]
                        else:
                            v = vpg[:, n % VR, pair * P:(pair + 1) * P]
                            a = ab[:, i % 3, (3 - x) * 64 + at:(3 - x) * 64 + at + 16]
                        last = pe.matmul(bank(4)[:, at:at + 16], v, a, start=(g < 0 and pair == 0), stop=(g == 3 and x == 3),
                                         skip_group_check=True)
                last.then_inc(s_bv, 1)

            pe.wait_ge(s_cst, 1)
            for t in range(TT):
                x_turn(t)
            norm(0)
            project((("qa", 3), ("ka", 3), ("va", 3)))
            pe.wait_ge(s_qk, 1)
            unit_emptied(pe, ("va", 4))
            unit_emptied(pe, ("va", 5))
            pe.wait_ge(s_nv, turn_base[("va", 2)] + 5)
            attend(("sw", "pw"))
            turn_outputs(sm_no[("pw", HPG - 1, 7)] + 1, 0)
            pe.wait_ge(s_Sr, sm_no[("pw", HPG - 1, 7)] + 1)
            pe.wait_ge(s_ote, SEQ // P)
            project((("qb", 2), ("kb", 2), ("vb", 2)))
            pe.wait_ge(s_qk, 2)
            unit_emptied(pe, ("vb", 2))
            unit_emptied(pe, ("vb", 3))
            pe.wait_ge(s_nv, turn_base[("vb", 1)] + 5)
            for i in range(AHEAD):
                sb_scores(i)
            for i in range(NS + 1):
                if i < NS:
                    sb_exponent(i)
                if i + AHEAD < NS:
                    sb_scores(i + AHEAD)
                if i >= 1:
                    sb_values(i - 1)
            pe.wait_ge(s_bo, len(outs_b))
            pe.wait_ge(s_ba, NS)
            for s in range(4):
                for c in range(2):
                    i = 2 * s + c
                    unit(("ga", i), column_tile(use_slot(("ga", s)), KT, SLOTW, c), hT)
                    unit(("ba", i), column_tile(use_slot(("br", s)), 2, SLOTW, c), oaT)
                    unit(("gb", i), column_tile(use_slot(("gb", s)), KT, SLOTW, c), hT)
                    unit(("bb", i), column_tile(use_slot(("br", s)), 4, SLOTW, c, 2 * SLOTW), obT)
                    x_turn(TT + i)
            x_turn(2 * TT - 1)
            pe.wait_ge(s_mg, KT)
            for i in range(KT):
                unit(("wo", i), column_tile(use_slot(("wo", i // 2)), KT, SLOTW, i % 2), mgT)
            for t in range(2):
                x_turn(2 * TT + t)
            norm(3, MEM)
            norm(1)
            for name in ("ck", "cv"):
                for i in range(2):
                    unit((name, i), column_tile(use_slot((name, 0)), KT, SLOTW, i), hmT, MEM,
                         normed=1 if (name, i) == ("ck", 0) else None)
            turn_rows(("ck", 0))
            turn_rows(("cv", 0))
            for i in range(2):
                unit(("cq", i), column_tile(use_slot(("cq", 0)), KT, SLOTW, i), hT, normed=None if i else 2)
            pe.wait_ge(s_qk, 3)
            unit_emptied(pe, ("cq", 0))
            unit_emptied(pe, ("cq", 1))
            pe.wait_ge(s_nv, 5 * len(turned) + 2)
            attend(("sx", "px"))
            turn_outputs(len(sm), SEQ // P)
            pe.wait_ge(s_ote, 2 * (SEQ // P))
            for i in range(KT):
                unit(("co", i), column_tile(use_slot(("co", 0)), 2, D, i), oaT)
            norm(2)
            for c in range(NC + 1):
                if c < NC:
                    high, low = split_slot(("up", c))
                    for i in range(2):
                        unit_split(("up", c, i), column_tile(high, KT, SLOTW, i), column_tile(low, KT, SLOTW, i), hTH, hTL,
                                   normed=None if c or i else 3)
                if c >= 1:
                    high, low = split_slot(("dn", c - 1))
                    pe.wait_ge(s_hl, 2 * c)
                    for i in range(KT):
                        unit_split(("dn", c - 1, i), column_tile(high, 2, D, i), column_tile(low, 2, D, i),
                                   hidH[:, (c - 1) % 2, :, :], hidL[:, (c - 1) % 2, :, :])
            norm(4)
            pe.wait_ge(s_h, KT * 5)
            for t in range(TT):
                if t >= 1:
                    pe.wait_ge(s_ye, t)
                n = P if t < TT - 1 else NEWK
                for k in range(KT):
                    last = pe.transpose(psum[0:n, 3072 + k * P:3072 + (k + 1) * P], xT[:, k, t * P:t * P + n], ident[:, :])
                last.then_inc(s_yt, 1)

        @block.scalar
        def _(act):
            chain = [0]

            def link(ins):
                chain[0] += 1
                ins.then_inc(s_aa, 1)
                act.wait_ge(s_aa, chain[0])

            def take(key, n=TOK):
                u = unit_no[key]
                act.wait_ge(s_lin, u + 1)
                return pieces(u, n)

            def x_evacuate(i):
                act.wait_ge(s_xt, i + 1)
                n = NEWK if i in (TT - 1, 2 * TT - 1) else P
                t = i % TT if i < 2 * TT else i - 2 * TT
                dst = (xT if i < 2 * TT else memT)[:, :, t * P:t * P + n]
                nc.scalar.copy(dst, psum[:, 3072:4096].rearrange("p (k n) -> p k n", k=KT)[:, :, 0:n]).then_inc(s_xe, 1)

            def norm(i, src, n=TOK):
                r = norm_order.index(i)
                sq, root = (sqb2, rb2) if i in (2, 4) else (sqb, rb)
                for k in range(KT):
                    if k >= 2:
                        act.wait_ge(s_squ, (KT - 1) * r + k - 1)
                    nc.scalar.activation(sq[:, k % 2, 0:n], src[:, k, 0:n], ACT.Square).then_inc(s_sq, 1)
                act.wait_ge(s_var, r + 1)
                nc.scalar.activation(root[:, 0:n], root[:, 0:n], ACT.Sqrt).then_inc(s_rt, 1)

            moves = [(i, b) for b in range(NB) for i in range(len(win_cache))]

            def move_windows(n):
                for i, b in moves[0:n]:
                    c = win_cache[i]
                    w = (c.shape[2] - NQ) * GW
                    act.dma_start(s_win[i][0, b].rearrange("k h d -> (k h d)")[0:w].rearrange("(a c) -> a c", a=32),
                                  c[0, b].rearrange("k h d -> (k h d)")[NQ * GW:].rearrange("(a c) -> a c", a=32)
                                  ).then_inc(s_mv, 16)
                del moves[0:n]

            def project(names):
                for name, n in names:
                    for i in range(2 * n):
                        move_windows(3)
                        if name[0] == "v" and i % 2 == 0:
                            if (name, i // 2) != ("va", 0):
                                k = (name, i // 2 - 1) if i else ("va", 2)
                                act.wait_ge(s_nt, turn_base[k] + 5)
                        ps = take((name, i))
                        if name[0] == "q":
                            dst = (qaT if name == "qa" else qbT)[:, i, :]
                            for p, fold in ps:
                                last = nc.scalar.mul(fold(dst), p, HD ** -0.5)
                        else:
                            dst = (kaT if name == "ka" else kbT)[:, i, :] if name[0] == "k" else vt[:, i % 2, :]
                            for p, fold in ps:
                                last = nc.scalar.copy(fold(dst), p)
                        last.then_inc(s_ea, 1)

            def turned_keys(i):
                n, tiles = turns[i]
                kts = ktw if n < NWC else ktx
                act.wait_ge(s_kt, i + 1)
                if i >= 2:
                    act.wait_ge(s_ktm, i - 1)
                w = 2 * P * len(tiles)
                at = 512 * (6 + i % 2)
                nc.scalar.copy(kts[:, i % 2, 0:w], psum[:, at:at + w]).then_inc(s_ktv, 1)

            def probabilities(u):
                act.wait_ge(s_nmax, u + 1)
                w = width(u)
                nc.scalar.activation(p_of(u)[:, 0:w], p_of(u)[:, 0:w], ACT.Exp, bias=nm[:, u:u + 1],
                                     accum_out=Zs[:, u:u + 1]).then_inc(s_p, 1)

            def quad_out(u, j):
                quad_evacuate(act, nc.scalar.copy, u, j)

            def attend(kinds):
                mine = [u for u, k in enumerate(sm) if k[0] in kinds]
                for u in mine:
                    if sm[u][0][0] == "s":
                        for i, (n, _) in enumerate(turns):
                            if chunks[n][0:2] == sm[u]:
                                turned_keys(i)
                    if sm[u][0][0] == "s":
                        probabilities(u)
                        for j in range(len(quads(u))):
                            quad_out(u, j)
                        continue
                    if sm[u - 2][0] == sm[u][0]:
                        for j in range(len(quads(u - 2))):
                            quad_out(u - 2, j)
                    probabilities(u)
                for u in mine[-2:]:
                    for j in range(len(quads(u))):
                        quad_out(u, j)

            for t in range(TT):
                x_evacuate(t)
            act.wait_ge(s_xe, TT)
            norm(0, xT)
            project((("qa", 3),))
            act.wait_ge(s_ts, 1)
            act.wait_ge(s_lines, 16 * 3)
            project((("ka", 3), ("va", 3)))
            nc.scalar.preload_act_table_set("natural_log_exp_and_others")
            attend(("sw", "pw"))
            project((("qb", 2), ("kb", 2), ("vb", 2)))

            def page_keys(n):
                act.wait_ge(s_bkt, n + 1)
                if n >= 2:
                    m = n - 2
                    if m % 4 < 3:
                        act.wait_ge(s_bku, 3 * (m // 4) + m % 4 + 1)
                    else:
                        act.wait_ge(s_bS, steps.index(("s", m // PAGES, (m % PAGES) // 4)) + 1)
                at = 512 * (6 + n % 2)
                nc.scalar.copy(ktp[:, n % 2, :], psum[:, at:at + 512]).then_inc(s_bktv, 1)

            def step_keys(i):
                s = steps[i]
                if s[0] == "s" and s[2] >= 0:
                    for x in range(4):
                        page_keys(s[1] * PAGES + 4 * s[2] + x)

            def logarithm(i):
                s = steps[i]
                n, w = rows(s), span(s)
                lo = lo_of(s) if s[0] == "p" else 0
                z = zb[0:n, i % 3, lo:lo + w]
                act.wait_ge(s_bz, i + 1)
                link(nc.scalar.activation(z, z, ACT.Exp))
                nc.scalar.activation(z, z, ACT.Ln, bias=1.0).then_inc(s_bl, 1)

            def weigh(i):
                s = steps[i]
                n, w = rows(s), span(s)
                lo = lo_of(s) if s[0] == "p" else 0
                act.wait_ge(s_bc, i + 1)
                if i >= 3:
                    act.wait_ge(s_bv, i - 2)
                bias = sbb[:, s[1]:s[1] + 1] if s[0] == "p" else 0.0
                nc.scalar.activation(ab[0:n, i % 3, lo:lo + w], sb_bank(i)[0:n, lo:lo + w], ACT.Exp, bias=bias).then_inc(s_ba, 1)

            for i in range(AHEAD):
                step_keys(i)
            logarithm(0)
            for i in range(NS):
                if i + 1 < NS:
                    logarithm(i + 1)
                weigh(i)
                if i + AHEAD < NS:
                    step_keys(i + AHEAD)
            act.wait_ge(s_bv, NS)
            act.wait_ge(s_bR, NS)
            act.wait_ge(s_out, 16 * V_ROW_STORES)
            for i in range(KT):
                for j, (g, b) in enumerate((("ga", "ba"), ("gb", "bb"))):
                    ps = take((g, i))
                    if i:
                        unit_emptied(act, (b, i - 1))
                        if j:
                            act.wait_ge(s_mg, i)
                    for p, fold in ps:
                        last = nc.scalar.activation(fold(sg[:, j, :]), p, ACT.Sigmoid)
                    last.then_inc(s_ea, 1)
                x_evacuate(TT + i)
            x_evacuate(2 * TT - 1)
            act.wait_ge(s_lin, unit_no[("wo", KT - 1)] + 1)
            for t in range(2):
                x_evacuate(2 * TT + t)
            act.wait_ge(s_xe, 2 * TT + 2)
            norm(3, memT, MEM)
            unit_emptied(act, ("wo", KT - 1))
            norm(1, xT)
            for name, dst in (("ck", kmT), ("cv", vmT)):
                for i in range(2):
                    nc.scalar.copy(dst[:, i, :], take((name, i), MEM)[0][0]).then_inc(s_ea, 1)
            for i in range(2):
                for p, fold in take(("cq", i)):
                    last = nc.scalar.mul(fold(qcT[:, i, :]), p, HD ** -0.5)
                last.then_inc(s_ea, 1)
            attend(("sx", "px"))
            unit_emptied(act, ("co", KT - 1))
            act.wait_ge(s_out, 16 * (V_ROW_STORES + 2))

            def split_weights(key):
                n = split_no[key]
                i = slot_of[key]
                act.wait_ge(s_w[i % RING], w_count[i])
                if n >= 2:
                    before = split_keys[n - 2]
                    act.wait_ge(s_lin, unit_no[(*before, 1 if before[0] == "up" else KT - 1)] + 1)
                nc.scalar.copy(wH[:, n % 2, :], ring[:, i % RING, :]).then_inc(s_wh, 1)

            split_weights(("up", 0))
            norm(2, xT)
            for k in range(KT):
                act.wait_ge(s_nf, k + 1)
                nc.scalar.copy(hTH[:, k, :], hs[:, k % 3, :]).then_inc(s_nh, 1)
            split_weights(("up", 1))
            for c in range(NC + 1):
                if c >= 1:
                    split_weights(("dn", c - 1))
                for i in range(2 if c < NC else 0):
                    if c or i:
                        act.wait_ge(s_hl, 2 * c + i)
                    for p, fold in take(("up", c, i)):
                        last = nc.scalar.activation(fold(hid), p, ACT.Relu)
                    last.then_inc(s_ea, 1)
                    act.wait_ge(s_hq, 2 * c + i + 1)
                    nc.scalar.copy(hidH[:, c % 2, i, :], hid[:, :]).then_inc(s_hh, 1)
                if 1 <= c < NC - 1:
                    split_weights(("up", c + 1))
            unit_emptied(act, ("dn", NC - 1, KT - 1))
            norm(4, xT)
            for t in range(TT):
                act.wait_ge(s_yt, t + 1)
                if t >= 2:
                    act.wait_ge(s_yo[t % 2], 16 * (t // 2))
                n = P if t < TT - 1 else NEWK
                nc.scalar.copy(yst[0:n, t % 2, :], psum[0:n, 3072:4096]).then_inc(s_ye, 1)

        @block.vector
        def _(dve):
            chain = [0]

            def link(ins):
                chain[0] += 1
                ins.then_inc(s_dv, 1)
                dve.wait_ge(s_dv, chain[0])

            def take(key, n=TOK):
                u = unit_no[key]
                dve.wait_ge(s_lin, u + 1)
                return pieces(u, n)

            def norm(i, gain, src, dst, n=TOK):
                r = norm_order.index(i)
                root = rb2 if i in (2, 4) else rb
                if r:
                    dve.wait_ge(s_h, KT * r)
                for p, fold in take(("nm", i), n):
                    last = nc.vector.tensor_scalar(fold(root), p, 1.0 / D, EPS, ALU.mult, ALU.add)
                last.then_inc(s_ev, 1)
                unit_emptied(dve, ("nm", i))
                nc.vector.reciprocal(root[:, 0:n], root[:, 0:n]).then_inc(s_var, 1)
                dve.wait_ge(s_rt, r + 1)
                if dst is None:
                    for k in range(KT + 1):
                        if k >= 3:
                            dve.wait_ge(s_h, KT * r + k - 2)
                        if k < KT:
                            nc.vector.scalar_tensor_tensor(out=hs[:, k % 3, :], in0=src[:, k, :], scalar=gains[:, gain, k:k + 1],
                                                           in1=root, op0=ALU.mult, op1=ALU.mult).then_inc(s_nf, 1)
                        if k >= 1:
                            dve.wait_ge(s_nh, k)
                            nc.vector.tensor_tensor(hTL[:, k - 1, :], hs[:, (k - 1) % 3, :], hTH[:, k - 1, :].bitcast(F32),
                                                    ALU.subtract).then_inc(s_h, 1)
                    return
                for k in range(KT):
                    nc.vector.scalar_tensor_tensor(out=dst[:, k, 0:n], in0=src[:, k, 0:n], scalar=gains[:, gain, k:k + 1],
                                                   in1=root[:, 0:n], op0=ALU.mult, op1=ALU.mult).then_inc(s_h, 1)

            def add_to_x(key, i):
                x = xT[:, i, :]
                for p, fold in take(key):
                    last = nc.vector.tensor_tensor(fold(x), p, fold(x), ALU.add)
                last.then_inc(s_ev, 1)

            def rows_in(key):
                name, s = key
                if name[0] == "k":
                    i = k_slots.index(key)
                    if i >= 2:
                        dve.wait_ge(s_kout[i % 2], 32 * (i // 2))
                    dst = kn[:, i % 2, :, :]
                elif name[0] == "v":
                    dst = (va if name == "va" else vb)[:, :, s * GW:(s + 1) * GW]
                else:
                    dst = kvn[:, 0 if name == "ck" else 1, :, :]
                for j in range(5 if name[0] != "c" else 1):
                    i = turn_base[key] + j
                    dve.wait_ge(s_nt, i + 1)
                    n, m = (P, 2) if 2 * j < TT - 1 else (NEWK, 1)
                    at = 512 * (6 + i % 2)
                    nc.vector.tensor_copy(dst[0:n, 2 * j:2 * j + m, :],
                                          psum[0:n, at:at + m * GW].rearrange("p (t n) -> p t n", t=m)).then_inc(s_nv, 1)

            def block_queries(src, dst, groups):
                for j in range(2 * groups):
                    for e in range(2):
                        c = (2 * (j % 2) + e) * NQ
                        last = nc.vector.tensor_copy(
                            dst[HD * e:HD * (e + 1), j, :, c:c + NQ],
                            src[HD * e:HD * (e + 1), j, SEQ:TOK].rearrange("p (b q) -> p b q", b=NB))
                last.then_inc(s_qk, 1)

            def scores(u):
                kind = sm[u][0]
                if kind[0] == "p":
                    if u >= 3:
                        dve.wait_ge(s_pt, quad_base[u - 2])
                else:
                    dve.wait_ge(s_pt, quad_base[u]) if quad_base[u] else None
                dve.wait_ge(s_S, u + 1)
                p = p_of(u)
                if kind == "sw":
                    hf = sm[u][1]
                    parts = [(0, OLDK, Ts), (OLDK, WINW, TsN[:, hf, :, :].rearrange("p g n -> p (g n)"))]
                elif kind == "pw":
                    h = sm[u][1]
                    dve.wait_ge(s_T, 48 * (h + 1))
                    parts, at = [], 0
                    for g in range(3):
                        n = min(REACH[g], sm[u][2] + 1) * P
                        parts.append((at, at + n, Th[:, SEG[g + 1] - n:SEG[g + 1]]))
                        at += n
                else:
                    parts = [(0, MEM, zeros)]
                for x, (a, b, t) in enumerate(parts):
                    last = nc.vector.tensor_tensor_reduce(out=p[:, a:b], in0=psum[:, a:b], in1=t, scale=1.0, scalar=LOW,
                                                          op0=ALU.add, op1=ALU.max, accum_out=mx[:, u, x:x + 1])
                last.then_inc(s_Sr, 1)
                dve.wait_ge(s_Sr, u + 1)
                link(nc.vector.tensor_reduce(nm[:, u:u + 1], mx[:, u, 0:len(parts)], AX.X, ALU.max))
                nc.vector.tensor_scalar(nm[:, u:u + 1], nm[:, u:u + 1], -1.0, None, ALU.mult).then_inc(s_nmax, 1)

            def quad_out(u, j):
                quad_evacuate(dve, nc.vector.tensor_copy, u, j)

            def reciprocal(u):
                dve.wait_ge(s_p, u + 1)
                link(nc.vector.reciprocal(rz[:, u:u + 1], Zs[:, u:u + 1]))

            def sample_unit(u):
                scores(u)
                reciprocal(u)
                w = width(u)
                p = p_of(u)[:, 0:w]
                nc.vector.tensor_scalar(p, p, rz[:, u:u + 1], None, ALU.mult).then_inc(s_pn, 1)
                for j in range(len(quads(u))):
                    quad_out(u, j)
                dve.wait_ge(s_o, u + 1)
                hf = sm[u][1]
                o = psum[:, 512 * (6 + u % 2):512 * (6 + u % 2) + P].rearrange("p (b j n) -> p j b n", b=4, j=2)
                for e in range(2):
                    for j in range(2):
                        last = nc.vector.tensor_copy(
                            oaT[HD * e:HD * (e + 1), j, SEQ + 32 * hf:SEQ + 32 * (hf + 1)].rearrange("p (b q) -> p b q", b=4),
                            o[HD * e:HD * (e + 1), j, :, NQ * e:NQ * (e + 1)])
                last.then_inc(s_oe, 1)

            def prompt_output(u, j0=0):
                _, h, t = sm[u]
                for j in range(j0, len(quads(u))):
                    quad_out(u, j)
                reciprocal(u)
                dve.wait_ge(s_o, u + 1)
                at = 512 * (6 + u % 2)
                nc.vector.tensor_scalar(onat[:, t, h * HD:(h + 1) * HD], psum[:, at:at + HD], rz[:, u:u + 1], None,
                                        ALU.mult).then_inc(s_oe, 1)

            def attend(kinds, n0):
                mine = [u for u, k in enumerate(sm) if k[0] in kinds]
                for u in mine:
                    if sm[u][0][0] == "s":
                        sample_unit(u)
                        continue
                    behind = u - 2 if sm[u - 2][0] == sm[u][0] else None
                    if behind is not None:
                        for j in range(min(2, len(quads(behind)))):
                            quad_out(behind, j)
                    scores(u)
                    if behind is not None:
                        prompt_output(behind, 2)
                prompt_output(mine[-2])
                prompt_output(mine[-1])
                for t in range(SEQ // P):
                    dve.wait_ge(s_ot, n0 + t + 1)
                    at = 512 * (4 + t % 2)
                    nc.vector.tensor_copy(oaT[:, :, t * P:(t + 1) * P],
                                          psum[:, at:at + 2 * P].rearrange("p (c n) -> p c n", c=2)).then_inc(s_ote, 1)

            dve.wait_ge(s_small, 16 * 7)
            link(nc.vector.memset(lines, NEG))
            for g, (_, d) in enumerate(GROUPS):
                for m0, m1, b in bucket_runs(d):
                    i0, i1 = NTAPS - m1, NTAPS - m0
                    last = nc.vector.tensor_copy(taps[:, g, i0:i1], relT[:, b:b + 1].to_broadcast([12, i1 - i0]))
            link(last)
            for g, (_, d) in enumerate(GROUPS):
                n = REACH[g] * P
                far = min(NTAPS - 1, (n - 1) // d)
                z0 = sum(LINE[:g]) + n - 1 - d * far
                last = nc.vector.tensor_copy(lines[:, z0:z0 + d * far + 1:d], taps[:, g, NTAPS - 1 - far:NTAPS])
            last.then_inc(s_taps, 1)
            for j in range(4):
                last = nc.vector.tensor_copy(brow[:, j, :].rearrange("o (h q) -> o h q", h=SBH),
                                             sbb[0:1, :].rearrange("o (h u) -> o h u", u=1).to_broadcast([1, SBH, NQ]))
            dve.wait_ge(s_cst, 1)
            link(nc.vector.tensor_reduce(oh, ohw.rearrange("p i r -> p r i"), AX.X, ALU.add))
            link(nc.vector.tensor_scalar(selr, oh, -1.0, -NEG, ALU.add, ALU.mult))
            link(nc.vector.memset(bsel, NEG))
            for hf in range(2):
                for b in range(4):
                    nc.vector.memset(bsel[32 * b:32 * b + 32, hf, 4 * hf + b:4 * hf + b + 1], 0.0)
            nc.vector.memset(RP1, NEG)
            link(nc.vector.memset(RP2, NEG))
            norm(0, 0, xT, hT)
            dve.wait_ge(s_trow, 16 * 17)
            nc.vector.tensor_copy(RP1[:, NQ:NQ + NTAPS], rowt[:, 0, :])
            link(nc.vector.tensor_copy(RP2[:, NQ:NQ + 4 * (NTAPS - 1) + 1:4], rowt[:, 1, :]))
            for t, rp, n in ((T1, RP1, P + NQ), (T2, RP2, 512 + NQ)):
                link(nc.vector.tensor_scalar(t, rp[:, NQ:NQ + n], oh[:, 0:1], None, ALU.mult))
                for q in range(1, NQ):
                    link(nc.vector.scalar_tensor_tensor(out=t, in0=rp[:, NQ - q:NQ - q + n], scalar=oh[:, q:q + 1], in1=t,
                                                        op0=ALU.mult, op1=ALU.add))
            dve.wait_ge(s_squ, 7)
            dve.wait_ge(s_h, KT)
            nc.vector.tensor_copy(Ts[:, 0:P], T1[:, 0:P])
            nc.vector.tensor_copy(Ts[:, P:P + 512].rearrange("p (r a) -> p r a", r=4),
                                  T2[:, 0:512].rearrange("p (a r) -> p r a", r=4))
            for r in range(NQ):
                nc.vector.tensor_scalar(Ts[:, 640 + r * P:640 + (r + 1) * P], rowt[:, 2, 0:P], selr[:, r:r + 1], None, ALU.add)
            link(nc.vector.tensor_scalar(nw3, selr, rowt[:, 2, NTAPS - 1:NTAPS], None, ALU.add))
            for hf in range(2):
                for g, row in enumerate((T1[:, P:P + NQ], T2[:, 512:512 + NQ], nw3)):
                    last = nc.vector.tensor_tensor(
                        TsN[:, hf, g, :].rearrange("p (b j) -> p b j", b=NB),
                        row.rearrange("p (u j) -> p u j", u=1).to_broadcast([P, NB, NQ]),
                        bsel[:, hf, :].rearrange("p (b u) -> p b u", u=1).to_broadcast([P, NB, NQ]), ALU.add)
            last.then_inc(s_ts, 1)
            unit_emptied(dve, ("qa", 5))
            block_queries(qaT, qblk, 3)
            for name in ("ka", "va"):
                for s in range(3):
                    rows_in((name, s))
            dve.wait_ge(s_ts, 1)
            dve.wait_ge(s_kout[0], 2 * 32)
            dve.wait_ge(s_kout[1], 32)
            attend(("sw", "pw"), 0)
            unit_emptied(dve, ("qb", 3))
            for e in range(2):
                for j in range(4):
                    last = nc.vector.tensor_copy(qbb[HD * e:HD * (e + 1), j, :, NQ * e:NQ * (e + 1)],
                                                 qbT[HD * e:HD * (e + 1), j, SEQ:TOK].rearrange("p (b q) -> p b q", b=NB))
            last.then_inc(s_qk, 1)
            for s in range(2):
                rows_in(("kb", s))
            dve.wait_ge(s_out, 16 * 6)
            for s in range(2):
                rows_in(("vb", s))
            dve.wait_ge(s_kout[0], 3 * 32)
            dve.wait_ge(s_kout[1], 2 * 32)

            def softplus(i):
                s = steps[i]
                n, w = rows(s), span(s)
                lo = lo_of(s) if s[0] == "p" else 0
                bias = sbb[:, s[1]:s[1] + 1] if s[0] == "p" else 0.0
                dve.wait_ge(s_bl, i + 1)
                if i >= 2:
                    dve.wait_ge(s_bc, i - 1)
                sp = spb[0:n, i % 2, lo:lo + w]
                ins = nc.vector.scalar_tensor_tensor(out=sp, in0=sb_bank(i)[0:n, lo:lo + w], scalar=bias,
                                                     in1=zb[0:n, i % 3, lo:lo + w], op0=ALU.add, op1=ALU.max)
                if needs_mask(s):
                    link(ins)
                    m, v = (below[:, :], sp[:, 0:P]) if s[0] == "p" else (newmask[:, s[1], :, :].rearrange("p h q -> p (h q)"), sp)
                    ins = nc.vector.tensor_tensor(v, v, m, ALU.mult)
                ins.then_inc(s_bsp, 1)

            def running(i):
                s = steps[i]
                w = span(s)
                before = earlier(i)
                dve.wait_ge(s_bsp, i + 1)
                if s[0] == "p":
                    lo, k = lo_of(s), place(i)
                    if before is None:
                        prev = max([x for x in range(i) if steps[x][0] == "p"], default=None)
                        if prev is not None:
                            dve.wait_ge(s_bc, prev + 1)
                        link(nc.vector.memset(Rp[:, :, :], 0.0))
                    else:
                        dve.wait_ge(s_bc, before + 1)
                        dve.wait_ge(s_bR, before + 1)
                    nc.vector.tensor_tensor(Rp[:, (k + 1) % 2, lo:512], Rp[:, k % 2, lo:512], spb[:, i % 2, lo:512],
                                            ALU.add).then_inc(s_bR, 1)
                    return
                g = s[2]
                if g < 0:
                    if i >= 1 and s[1] > 0:
                        dve.wait_ge(s_bc, last_of[("s", s[1] - 1)] + 1)
                    link(nc.vector.memset(Rs[:, 0, 4, :], 0.0))
                    nc.vector.tensor_copy(Rs[0:NEWK, 0, 4, :], spb[0:NEWK, i % 2, 0:64]).then_inc(s_bR, 1)
                    return
                dve.wait_ge(s_bc, before + 1)
                dve.wait_ge(s_bR, before + 1)
                for x in range(3, -1, -1):
                    dst = Rs[:, g % 2, x, :] if x else Rs[:, (g + 1) % 2, 4, :]
                    ins = nc.vector.tensor_tensor(dst, Rs[:, g % 2, x + 1, :], spb[:, i % 2, 64 * x:64 * (x + 1)], ALU.add)
                    if x:
                        link(ins)
                ins.then_inc(s_bR, 1)

            def output(i):
                if i not in out_no:
                    return
                s = steps[i]
                dve.wait_ge(s_bv, i + 1)
                if s[0] == "p":
                    _, h, c, _ = s
                    hp = HD * (h % 2)
                    nc.vector.tensor_copy(obT[hp:hp + HD, h // 2, c * 512:(c + 1) * 512],
                                          bank(3)[hp:hp + HD, :]).then_inc(s_bo, 1)
                    return
                o = bank(4)[:, 0:64].rearrange("p (j n) -> p j n", j=4)
                for e in range(2):
                    last = nc.vector.tensor_copy(obT[HD * e:HD * (e + 1), :, SEQ + NQ * s[1]:SEQ + NQ * (s[1] + 1)],
                                                 o[HD * e:HD * (e + 1), :, NQ * e:NQ * (e + 1)])
                last.then_inc(s_bo, 1)

            def clamp(i):
                s = steps[i]
                n, w = rows(s), span(s)
                lo = lo_of(s) if s[0] == "p" else 0
                bias = sbb[:, s[1]:s[1] + 1] if s[0] == "p" else 0.0
                dve.wait_ge(s_bS, i + 1)
                nc.vector.tensor_scalar(zb[0:n, i % 3, lo:lo + w], sb_bank(i)[0:n, lo:lo + w], bias, BIG, ALU.add,
                                        ALU.min).then_inc(s_bz, 1)

            clamp(0)
            clamp(1)
            for i in range(NS + 2):
                if i < NS:
                    softplus(i)
                    running(i)
                if i + 2 < NS:
                    clamp(i + 2)
                if i >= 2:
                    output(i - 2)
            for i in range(KT):
                ps = take(("ba", i))
                unit_emptied(dve, ("ga", i))
                for p, fold in ps:
                    last = nc.vector.tensor_tensor(fold(mgT[:, i, :]), p, fold(sg[:, 0, :]), ALU.mult)
                last.then_inc(s_ev, 1)
                ps = take(("bb", i))
                unit_emptied(dve, ("gb", i))
                for p, fold in ps:
                    last = nc.vector.tensor_tensor(fold(sg[:, 1, :]), p, fold(sg[:, 1, :]), ALU.mult)
                last.then_inc(s_ev, 1)
                unit_emptied(dve, ("bb", i))
                nc.vector.tensor_tensor(mgT[:, i, :], mgT[:, i, :], sg[:, 1, :], ALU.add).then_inc(s_mg, 1)
            dve.wait_ge(s_xe, 2 * TT)
            for i in range(KT):
                add_to_x(("wo", i), i)
            nc.vector.memset(zeros, 0.0)
            link(nc.vector.memset(qcb, 0.0))
            norm(3, 3, memT, hmT, MEM)
            norm(1, 1, xT, hT)
            rows_in(("ck", 0))
            rows_in(("cv", 0))
            unit_emptied(dve, ("cq", 1))
            block_queries(qcT, qcb, 1)
            attend(("sx", "px"), SEQ // P)
            for i in range(KT):
                add_to_x(("co", i), i)
            def split_weights(key):
                n = split_no[key]
                dve.wait_ge(s_wh, n + 1)
                nc.vector.tensor_tensor(wL[:, n % 2, :], ring[:, slot_of[key] % RING, :], wH[:, n % 2, :].bitcast(F32),
                                        ALU.subtract).then_inc(s_wl, 1)

            split_weights(("up", 0))
            norm(2, 2, xT, None)
            split_weights(("up", 1))
            for c in range(NC + 1):
                if 1 <= c < NC:
                    split_weights(("dn", c - 1))
                for i in range(2 if c < NC else 0):
                    unit_emptied(dve, ("up", c, i))
                    nc.vector.tensor_tensor(hid[:, :], hid[:, :], hid[:, :], ALU.mult).then_inc(s_hq, 1)
                    dve.wait_ge(s_hh, 2 * c + i + 1)
                    nc.vector.tensor_tensor(hidL[:, c % 2, i, :], hid[:, :], hidH[:, c % 2, i, :].bitcast(F32),
                                            ALU.subtract).then_inc(s_hl, 1)
                for i in range(KT if c >= 1 else 0):
                    add_to_x(("dn", c - 1, i), i)
                    if i == 3 and c < NC:
                        split_weights(("up", c + 1) if c + 1 < NC else ("dn", NC - 1))
            norm(4, 4, xT, xT)


_INS = ["x_prompt", "x_sample", "mem_prompt", "cache_win1_k", "cache_win1_v", "cache_win2_k", "cache_win2_v",
        "cache_win3_k", "cache_win3_v", "cache_sb_k", "cache_sb_v", "cache_mem_k", "cache_mem_v", "page_table",
        "norm_mix", "w_in", "w_branch_a", "w_branch_b", "w_out", "rel_bias", "sb_bias", "norm_cross", "norm_mem",
        "w_cq", "w_ck", "w_cv", "w_co", "norm_mlp", "w_up", "w_down", "norm_final"]
_OUTS = [(1, SEQ, D), (NB, NQ, D)]
_OUTS += [(1, 1, min(w, SEQ), HPG, HD) for w, _ in GROUPS for _ in range(2)]
_OUTS += [(1, 1, SEQ, SBH, HD)] * 2 + [(1, 1, MEM, HPG, HD)] * 2
_OUTS += [(1, NB, w, HPG, HD) for w, _ in GROUPS for _ in range(2)]
_OUTS += [(1, NB, NQ, SBH, HD)] * 2


def kernel(**inputs):
    import concourse.bacc as _bacc
    from concourse import mybir as _mybir
    from concourse.bass_utils import run_bass_kernel_spmd as _run

    nc = _bacc.Bacc("TRN2", target_bir_lowering=False, num_devices=1)
    arrays, ins, outs = {}, [], []
    for name in _INS:
        a = np.ascontiguousarray(inputs[name])
        arrays[f"in_{name}"] = a
        ins.append(nc.dram_tensor(f"in_{name}", a.shape, _mybir.dt.from_np(a.dtype), kind="ExternalInput").ap())
    for i, shape in enumerate(_OUTS):
        outs.append(nc.dram_tensor(f"out_{i}", shape, F32, kind="ExternalOutput").ap())
    scratch = (nc.dram_tensor("bias_lines", (12, 1152), F32).ap(), nc.dram_tensor("tap_rows", (12, 3, NTAPS), F32).ap(),
               nc.dram_tensor("line_copies", (12, P, 1152), F32).ap())
    hybrid_decoder_kernel(nc, ins, outs, scratch)
    r = _run(nc, [arrays], core_ids=[0])
    return tuple(r.results[0][f"out_{i}"] for i in range(len(_OUTS)))
```
